# Optimizing a Trainium2 kernel written in Bass

```python
import math
import jax, jax.numpy as jnp
from jax import lax
import numpy as np

D_MODEL = 1024
BATCH = 1
SEQ = 512
DEPTH = 2

QBLK = 128
SB_HEADS = 8
SB_HEAD_DIM = 64
SB_WIDTH = SB_HEADS * SB_HEAD_DIM
SSM_HEADS = 16
SSM_HEAD_DIM = 64
SSM_INNER = SSM_HEADS * SSM_HEAD_DIM
SSM_GROUPS = 4
SSM_STATE = 128
SSM_CONV = 4
SSM_CHUNK = 128
SSM_CONV_DIM = SSM_INNER + 2 * SSM_GROUPS * SSM_STATE
DT_MIN = 1e-3
DT_MAX = 0.1
NSA_HEADS = 16
NSA_KV_GROUPS = 4
NSA_HEAD_DIM = 64
NSA_Q = NSA_HEADS * NSA_HEAD_DIM
NSA_KV = NSA_KV_GROUPS * NSA_HEAD_DIM
CMP_BLOCK = 32
CMP_STRIDE = 16
CMP_HIDDEN = 256
SEL_BLOCK = 64
N_SEL = 16
WINDOW = 512
N_BRANCH = 3
REL_BUCKETS = 32
REL_MAX_EXACT = 16
REL_MAX_DIST = 1024
D_FF = 2816
FFN_CONV = 3

EPS = 1e-6
NEG = -1e30
FORCE = 1e4
N_EVEN = (DEPTH + 1) // 2
N_ODD = DEPTH // 2
AB_IN = 3 * SB_WIDTH + SSM_INNER + SSM_CONV_DIM + SSM_HEADS
AB_MIX = SB_WIDTH + SSM_INNER
NSA_IN = NSA_Q + 6 * NSA_KV + NSA_HEADS * N_BRANCH

kernel_name = "hybrid_sb_ssd_nsa_convffn_trunk"

def rmsnorm(x, g):
    xf = x.astype(jnp.float32)
    y = xf * lax.rsqrt(jnp.mean(xf * xf, axis=-1, keepdims=True) + EPS)
    return (y * g.astype(jnp.float32)).astype(x.dtype)

def causal_dwconv(x, w, b):
    k_len, ch = w.shape
    y = lax.conv_general_dilated(x, w[:, None, :].astype(x.dtype), window_strides=(1,),
                                 padding=[(k_len - 1, 0)],
                                 dimension_numbers=("NWC", "WIO", "NWC"),
                                 feature_group_count=ch)
    return y + b.astype(x.dtype)

def rel_bucket(n):
    n = jnp.maximum(n, 0)
    nf = jnp.maximum(n, 1).astype(jnp.float32)
    large = REL_MAX_EXACT + (jnp.log(nf / REL_MAX_EXACT) / math.log(REL_MAX_DIST / REL_MAX_EXACT)
                             * (REL_BUCKETS - REL_MAX_EXACT)).astype(jnp.int32)
    large = jnp.minimum(large, REL_BUCKETS - 1)
    return jnp.where(n < REL_MAX_EXACT, n, large)

def masked_softmax(logits, mask):
    logits = jnp.where(mask, logits.astype(jnp.float32), NEG)
    return jnp.where(mask, jax.nn.softmax(logits, axis=-1), 0.0)

def stick_breaking(q, k, v):
    b, h, s, d = q.shape
    scale = d ** -0.5
    kpos = jnp.arange(s)

    def block(i):
        q0 = i * QBLK
        qb = lax.dynamic_slice_in_dim(q, q0, QBLK, axis=2)
        z = jnp.einsum("bhqd,bhkd->bhqk", qb, k).astype(jnp.float32) * scale
        t = q0 + jnp.arange(QBLK)
        mask = kpos[None, :] < t[:, None]
        log_rest = jnp.where(mask, jax.nn.log_sigmoid(-z), 0.0)
        suffix = lax.cumsum(log_rest, axis=3, reverse=True) - log_rest
        w = jnp.where(mask, jnp.exp(jax.nn.log_sigmoid(z) + suffix), 0.0)
        return jnp.einsum("bhqk,bhkd->bhqd", w.astype(v.dtype), v)

    o = lax.map(block, jnp.arange(s // QBLK))
    return o.transpose(1, 2, 0, 3, 4).reshape(b, h, s, d)

def ssd(x, dt, a_neg, bm, cm):
    b, s, h, p = x.shape
    g, n = bm.shape[2], bm.shape[3]
    hg = h // g
    ln = SSM_CHUNK
    nc = s // ln
    a = (dt * a_neg).reshape(b, nc, ln, g, hg)
    xdt = (x.astype(jnp.float32) * dt[..., None]).reshape(b, nc, ln, g, hg, p)
    bc = bm.astype(jnp.float32).reshape(b, nc, ln, g, n)
    cc = cm.astype(jnp.float32).reshape(b, nc, ln, g, n)
    a_cs = jnp.cumsum(a, axis=2)
    causal = jnp.tril(jnp.ones((ln, ln), dtype=bool))
    seg = a_cs[:, :, :, None] - a_cs[:, :, None]
    decay = jnp.exp(jnp.where(causal[None, None, :, :, None, None], seg, NEG))
    cb = jnp.einsum("bclgn,bcsgn->bclsg", cc, bc)
    y_diag = jnp.einsum("bclsg,bclsgh,bcsghp->bclghp", cb, decay, xdt)
    decay_out = jnp.exp(a_cs[:, :, -1:] - a_cs)
    states = jnp.einsum("bcsgn,bcsgh,bcsghp->bcghpn", bc, decay_out, xdt)
    chunk_decay = jnp.exp(a_cs[:, :, -1])

    def step(h_prev, inp):
        dec, st = inp
        return dec[..., None, None] * h_prev + st, h_prev

    h0 = jnp.zeros((b, g, hg, p, n), jnp.float32)
    _, prev = lax.scan(step, h0, (chunk_decay.transpose(1, 0, 2, 3), states.transpose(1, 0, 2, 3, 4, 5)))
    prev = prev.transpose(1, 0, 2, 3, 4, 5)
    y_off = jnp.einsum("bclgn,bcghpn,bclgh->bclghp", cc, prev, jnp.exp(a_cs))
    return (y_diag + y_off).reshape(b, s, h, p)

def mixer_ab(h, w_in, conv_w, conv_b, dt_bias, a_log, d_skip, ssm_norm, w_out):
    b, s, _ = h.shape
    proj = h @ w_in
    o3 = 3 * SB_WIDTH
    q, k, v, z, xbc, dt_raw = jnp.split(
        proj, [SB_WIDTH, 2 * SB_WIDTH, o3, o3 + SSM_INNER, o3 + SSM_INNER + SSM_CONV_DIM], axis=-1)
    heads = lambda t: t.reshape(b, s, SB_HEADS, SB_HEAD_DIM).transpose(0, 2, 1, 3)
    o_sb = stick_breaking(heads(q), heads(k), heads(v)).transpose(0, 2, 1, 3).reshape(b, s, SB_WIDTH)
    xbc = jax.nn.silu(causal_dwconv(xbc, conv_w, conv_b))
    xs, bm, cm = jnp.split(xbc, [SSM_INNER, SSM_INNER + SSM_GROUPS * SSM_STATE], axis=-1)
    dt = jax.nn.softplus(dt_raw.astype(jnp.float32) + dt_bias.astype(jnp.float32))
    a_neg = -jnp.exp(a_log.astype(jnp.float32))
    xs_h = xs.reshape(b, s, SSM_HEADS, SSM_HEAD_DIM)
    y = ssd(xs_h, dt, a_neg, bm.reshape(b, s, SSM_GROUPS, SSM_STATE), cm.reshape(b, s, SSM_GROUPS, SSM_STATE))
    y = y + xs_h.astype(jnp.float32) * d_skip.astype(jnp.float32)[:, None]
    y = y.reshape(b, s, SSM_INNER)
    y = rmsnorm(y * jax.nn.silu(z.astype(jnp.float32)), ssm_norm).astype(h.dtype)
    return jnp.concatenate([o_sb.astype(h.dtype), y], axis=-1) @ w_out

def compress(kv, pe, w1, b1, w2):
    b, s, g, d = kv.shape
    halves = kv.reshape(b, s // CMP_STRIDE, CMP_STRIDE, g, d)
    blocks = jnp.concatenate([halves[:, :-1], halves[:, 1:]], axis=2)
    blocks = blocks + pe[None, None, :, None, :]
    flat = blocks.transpose(0, 1, 3, 2, 4).reshape(b, s // CMP_STRIDE - 1, g, CMP_BLOCK * d)
    return jax.nn.silu(flat @ w1 + b1) @ w2

def mixer_nsa(h, rel_bias, w_in, cmp_w1, cmp_b1, cmp_w2, cmp_pe, w_out):
    b, s, _ = h.shape
    g, hg, d = NSA_KV_GROUPS, NSA_HEADS // NSA_KV_GROUPS, NSA_HEAD_DIM
    proj = h @ w_in
    parts = jnp.split(proj, [NSA_Q + i * NSA_KV for i in range(7)], axis=-1)
    q = parts[0].reshape(b, s, g, hg, d)
    kc, vc, ksl, vsl, kw, vw = [t.reshape(b, s, g, d) for t in parts[1:7]]
    gates = jax.nn.sigmoid(parts[7].astype(jnp.float32)).reshape(b, s, g, hg, N_BRANCH)
    kcmp = compress(kc, cmp_pe[0], cmp_w1[0], cmp_b1[0], cmp_w2[0])
    vcmp = compress(vc, cmp_pe[1], cmp_w1[1], cmp_b1[1], cmp_w2[1])
    nc = kcmp.shape[1]
    ns = s // SEL_BLOCK
    n_sel = min(N_SEL, ns)
    cmp_end = CMP_STRIDE * jnp.arange(nc) + CMP_BLOCK - 1
    ci = (jnp.arange(nc) * CMP_STRIDE)[:, None]
    sj = (jnp.arange(ns) * SEL_BLOCK)[None, :]
    overlap = ((ci < sj + SEL_BLOCK) & (ci + CMP_BLOCK > sj)).astype(jnp.float32)
    ks_blk = ksl.reshape(b, ns, SEL_BLOCK, g, d).transpose(0, 3, 1, 2, 4)
    vs_blk = vsl.reshape(b, ns, SEL_BLOCK, g, d).transpose(0, 3, 1, 2, 4)
    kw_pad = jnp.pad(kw, ((0, 0), (WINDOW, 0), (0, 0), (0, 0)))
    vw_pad = jnp.pad(vw, ((0, 0), (WINDOW, 0), (0, 0), (0, 0)))
    bias_gh = rel_bias.reshape(g, hg, REL_BUCKETS)
    bias_t = bias_gh.transpose(0, 2, 1)
    b_ix = jnp.arange(b)[:, None, None, None]
    g_ix = jnp.arange(g)[None, :, None, None]
    jj = jnp.arange(ns)
    scale = d ** -0.5

    def block(i):
        q0 = i * QBLK
        t = q0 + jnp.arange(QBLK)
        qb = lax.dynamic_slice_in_dim(q, q0, QBLK, axis=1).transpose(0, 2, 3, 1, 4)
        lc = (jnp.einsum("bghqd,bngd->bghqn", qb, kcmp).astype(jnp.float32) * scale
              + bias_gh[:, :, rel_bucket(t[:, None] - cmp_end[None])])
        pc = masked_softmax(lc, cmp_end[None] <= t[:, None])
        oc = jnp.einsum("bghqn,bngd->bghqd", pc.astype(vcmp.dtype), vcmp)
        imp = jnp.einsum("bghqn,nj->bgqj", pc, overlap)
        cur = t // SEL_BLOCK
        valid = (jj[None] * SEL_BLOCK) <= t[:, None]
        forced = (jj[None] == 0) | (jj[None] == cur[:, None]) | (jj[None] == cur[:, None] - 1)
        imp = jnp.where(forced, FORCE, jnp.where(valid, imp, -1.0))
        _, idx = lax.top_k(imp, n_sel)
        ksel = ks_blk[b_ix, g_ix, idx].reshape(b, g, QBLK, n_sel * SEL_BLOCK, d)
        vsel = vs_blk[b_ix, g_ix, idx].reshape(b, g, QBLK, n_sel * SEL_BLOCK, d)
        pos = (idx[..., None] * SEL_BLOCK + jnp.arange(SEL_BLOCK)).reshape(b, g, QBLK, n_sel * SEL_BLOCK)
        rel = t[:, None] - pos
        bias_s = jnp.moveaxis(bias_t[g_ix, rel_bucket(rel)], -1, 2)
        ls = jnp.einsum("bghqd,bgqkd->bghqk", qb, ksel).astype(jnp.float32) * scale + bias_s
        ps = masked_softmax(ls, (rel >= 0)[:, :, None])
        osl = jnp.einsum("bghqk,bgqkd->bghqd", ps.astype(vsel.dtype), vsel)
        kwb = lax.dynamic_slice_in_dim(kw_pad, q0, QBLK + WINDOW, axis=1)
        vwb = lax.dynamic_slice_in_dim(vw_pad, q0, QBLK + WINDOW, axis=1)
        spos = q0 - WINDOW + jnp.arange(QBLK + WINDOW)
        relw = t[:, None] - spos[None]
        lw = (jnp.einsum("bghqd,bkgd->bghqk", qb, kwb).astype(jnp.float32) * scale
              + bias_gh[:, :, rel_bucket(relw)])
        pw = masked_softmax(lw, (relw >= 0) & (relw < WINDOW) & (spos[None] >= 0))
        ow = jnp.einsum("bghqk,bkgd->bghqd", pw.astype(vwb.dtype), vwb)
        gb = lax.dynamic_slice_in_dim(gates, q0, QBLK, axis=1).transpose(0, 2, 3, 1, 4)
        o = gb[..., 0:1] * oc + gb[..., 1:2] * osl + gb[..., 2:3] * ow
        return o.transpose(0, 3, 1, 2, 4).reshape(b, QBLK, NSA_Q).astype(h.dtype)

    o = lax.map(block, jnp.arange(s // QBLK))
    o = o.transpose(1, 0, 2, 3).reshape(b, s, NSA_Q)
    return o @ w_out

def conv_ffn(h, w_up, conv_w, conv_b, w_down):
    u = causal_dwconv(h @ w_up, conv_w, conv_b)
    gate, val = jnp.split(u, 2, axis=-1)
    return (jax.nn.gelu(gate, approximate=True) * val) @ w_down

def setup_inputs(seed: int = 0) -> dict:
    key = jax.random.key(seed)
    ks = jax.random.split(key, 24)

    def nrm(k, shape, scale):
        return jax.random.normal(k, shape, jnp.float32) * scale

    dt0 = jnp.exp(jax.random.uniform(ks[9], (N_EVEN, SSM_HEADS), jnp.float32)
                  * (math.log(DT_MAX) - math.log(DT_MIN)) + math.log(DT_MIN))
    return {
        "x": nrm(ks[0], (BATCH, SEQ, D_MODEL), 1.0),
        "c": nrm(ks[1], (BATCH, D_MODEL), 1.0),
        "rel_bias": nrm(ks[2], (NSA_HEADS, REL_BUCKETS), 0.5),
        "ada_w": nrm(ks[3], (DEPTH, D_MODEL, 6 * D_MODEL), D_MODEL ** -0.5),
        "ada_b": nrm(ks[4], (DEPTH, 6 * D_MODEL), 0.01),
        "norm_g": 1.0 + nrm(ks[5], (DEPTH, 4, D_MODEL), 0.05),
        "ab_w_in": nrm(ks[6], (N_EVEN, D_MODEL, AB_IN), D_MODEL ** -0.5),
        "ab_conv_w": nrm(ks[7], (N_EVEN, SSM_CONV, SSM_CONV_DIM), SSM_CONV ** -0.5),
        "ab_conv_b": nrm(ks[8], (N_EVEN, SSM_CONV_DIM), 0.01),
        "ab_dt_bias": dt0 + jnp.log(-jnp.expm1(-dt0)),
        "ab_a_log": jnp.log(jax.random.uniform(ks[10], (N_EVEN, SSM_HEADS), jnp.float32, 1.0, 16.0)),
        "ab_d_skip": 1.0 + nrm(ks[11], (N_EVEN, SSM_HEADS), 0.1),
        "ab_ssm_norm": 1.0 + nrm(ks[12], (N_EVEN, SSM_INNER), 0.05),
        "ab_w_out": nrm(ks[13], (N_EVEN, AB_MIX, D_MODEL), AB_MIX ** -0.5),
        "nsa_w_in": nrm(ks[14], (N_ODD, D_MODEL, NSA_IN), D_MODEL ** -0.5),
        "nsa_cmp_w1": nrm(ks[15], (N_ODD, 2, CMP_BLOCK * NSA_HEAD_DIM, CMP_HIDDEN), (CMP_BLOCK * NSA_HEAD_DIM) ** -0.5),
        "nsa_cmp_b1": nrm(ks[16], (N_ODD, 2, CMP_HIDDEN), 0.01),
        "nsa_cmp_w2": nrm(ks[17], (N_ODD, 2, CMP_HIDDEN, NSA_HEAD_DIM), CMP_HIDDEN ** -0.5),
        "nsa_cmp_pe": nrm(ks[18], (N_ODD, 2, CMP_BLOCK, NSA_HEAD_DIM), 0.02),
        "nsa_w_out": nrm(ks[19], (N_ODD, NSA_Q, D_MODEL), NSA_Q ** -0.5),
        "ffn_w_up": nrm(ks[20], (DEPTH, D_MODEL, 2 * D_FF), D_MODEL ** -0.5),
        "ffn_conv_w": nrm(ks[21], (DEPTH, FFN_CONV, 2 * D_FF), FFN_CONV ** -0.5),
        "ffn_conv_b": nrm(ks[22], (DEPTH, 2 * D_FF), 0.01),
        "ffn_w_down": nrm(ks[23], (DEPTH, D_FF, D_MODEL), D_FF ** -0.5),
    }

def reference(x, c, rel_bias, ada_w, ada_b, norm_g, ab_w_in, ab_conv_w, ab_conv_b, ab_dt_bias,
              ab_a_log, ab_d_skip, ab_ssm_norm, ab_w_out, nsa_w_in, nsa_cmp_w1, nsa_cmp_b1,
              nsa_cmp_w2, nsa_cmp_pe, nsa_w_out, ffn_w_up, ffn_conv_w, ffn_conv_b, ffn_w_down):
    mod = (jnp.einsum("bd,lde->lbe", jax.nn.silu(c), ada_w) + ada_b[:, None, :])[:, :, None, :]
    for l in range(DEPTH):
        shift1, scale1, gate1, shift2, scale2, gate2 = jnp.split(mod[l], 6, axis=-1)
        h = rmsnorm(x, norm_g[l, 0]) * (1.0 + scale1) + shift1
        if l % 2 == 0:
            e = l // 2
            out = mixer_ab(h, ab_w_in[e], ab_conv_w[e], ab_conv_b[e], ab_dt_bias[e], ab_a_log[e],
                           ab_d_skip[e], ab_ssm_norm[e], ab_w_out[e])
        else:
            o = l // 2
            out = mixer_nsa(h, rel_bias, nsa_w_in[o], nsa_cmp_w1[o], nsa_cmp_b1[o], nsa_cmp_w2[o],
                            nsa_cmp_pe[o], nsa_w_out[o])
        x = x + gate1 * rmsnorm(out, norm_g[l, 1])
        h = rmsnorm(x, norm_g[l, 2]) * (1.0 + scale2) + shift2
        x = x + gate2 * rmsnorm(conv_ffn(h, ffn_w_up[l], ffn_conv_w[l], ffn_conv_b[l], ffn_w_down[l]), norm_g[l, 3])
    return x


_drawn_inputs = setup_inputs


def setup_inputs(seed=0):
    import zlib

    import numpy as np

    out = dict(_drawn_inputs(seed))
    spreads = {}
    factors = {'ab_conv_b': 8.0, 'nsa_cmp_b1': 31.423, 'nsa_cmp_pe': 8.0, 'ffn_conv_b': 8.0}
    for name, (base, spread) in spreads.items():
        noise = np.random.default_rng([zlib.crc32(name.encode()), seed]).standard_normal(out[name].shape)
        drawn = base * np.exp(spread * noise) if base else spread * noise
        out[name] = __import__('jax').numpy.asarray(drawn.astype(out[name].dtype))
    for name, factor in factors.items():
        out[name] = (out[name] * factor).astype(out[name].dtype)
    return out
```

```python
from contextlib import ExitStack

import concourse.bass as bass
from concourse import mybir

P = 128
F32 = mybir.dt.float32
F32R = mybir.dt.float32r
ALU = mybir.AluOpType
ACT = mybir.ActivationFunctionType

SEQ, DM = 512, 1024
NT = SEQ // P
KT = DM // P
SB_HEADS, HD = 8, 64
SSM_HEADS, SSM_GROUPS, SSM_INNER, SSM_STATE = 16, 4, 1024, 128
NSA_HEADS, NSA_GROUPS = 16, 4
CMP_N = SEQ // 16 - 1
D_FF = 2816
FT = D_FF // P
REL_BUCKETS = 32
EPS = 1e-6
NEG = -1e30
CH = 16
CW = CH * P
ADA_W = 256
ADA_N = 6 * DM // ADA_W
ADA_FIRST = 2 * DM // ADA_W
UB = SEQ + 4
PAD = 4
KOFF = (0, 512, 1024, 896)
QOFF = (512, 1024, 640, 0)
BANKS = ((0, 512), (512, 512), (1024, 256))


def param_columns():
    sizes = [("ada_b", 96), ("norm_g", 64), ("conv_w", 64), ("conv_b", 16), ("d_skip", 8), ("ssm_norm", 8),
             ("fconv_w0", 132), ("fconv_w1", 132), ("fconv_b0", 44), ("fconv_b1", 44),
             ("dt_bias", 16), ("a_log", 16), ("cond", 8)]
    at, cols = 0, {}
    for name, n in sizes:
        cols[name] = (at, n)
        at += n
    return cols, at


def nsa_columns():
    sizes = [("w2k", 256), ("w2v", 128), ("w_gate", 384), ("pe", 32), ("b1", 4)]
    at, cols = 0, {}
    for name, n in sizes:
        cols[name] = (at, n)
        at += n
    return cols, at


def chunk_plan():
    rows = [("v0", 2, 16, 0), ("q", 2, 16, 2), ("k", 2, 16, 2), ("xbc", 8, 16, 2), ("z", 4, 16, 2),
            ("out0", 8, 12, 1), ("up0", 22, 16, 2), ("down0", 16, 11, 1),
            ("v1", 2, 16, 0), ("f1", 8, 16, 2), ("w1", 4, 16, 1), ("out1", 4, 16, 2),
            ("up1", 22, 16, 2), ("down1", 16, 11, 1)]
    tiles = {"v0": 4, "v1": 4, "w1": 4, "down0": 8, "down1": 8}
    plan, c, ev, tile, extra = {}, 0, 0, 0, 0
    for name, n, size, per in rows:
        plan[name] = dict(c0=c, n=n, size=size, per=per, ev0=ev, t0=tile, extra=extra)
        c += n
        ev += n * per if per else 5
        tile += tiles.get(name, n * per)
        if size < CH and name != "down1":
            extra += 1
    return plan, [r[0] for r in rows]


def trunk(nc, x_t, consts, params, nsa_params, w_dt, onehot, relb, ada, w_v0, w_f0, w_out0, w_v1, w_f1, w_c1,
          w_out1, w_up, w_down, out_t):
    plan, order = chunk_plan()
    pcol, NP = param_columns()
    ncol, NN = nsa_columns()
    weights = {"v0": (w_v0, 0), "q": (w_f0, 0), "k": (w_f0, 2), "xbc": (w_f0, 4), "z": (w_f0, 12),
               "out0": (w_out0, 0), "up0": (w_up, 0), "down0": (w_down, 0), "v1": (w_v1, 0), "f1": (w_f1, 0),
               "w1": (w_c1, 0), "out1": (w_out1, 0), "up1": (w_up, 22), "down1": (w_down, 16)}

    ctx = ExitStack()
    with ctx:
        start = -(-nc.sbuf_base // 64) * 64
        top = [0]

        def at(name, shape, dt, offset):
            n = 4
            for d in shape[1:]:
                n *= d
            top[0] = max(top[0], offset + n)
            return nc.alloc_sbuf_tensor_at(name, shape, dt, offset=offset)

        o = start
        fixed = {}
        for name, shape, dt in [
            ("x", [P, KT, SEQ], F32), ("raw", [P, 2, CW], F32), ("ring", [P, 2, 2, CW], F32R),
            ("cf", [P, 4, P], F32), ("cr", [P, 5, P], F32R), ("par", [P, NP], F32), ("modc", [P, 96], F32),
            ("gains", [P, 64], F32), ("cond", [P, KT], F32), ("one", [P, 1], F32),
        ]:
            fixed[name] = at(name, shape, dt, o)
            n = 4
            for d in shape[1:]:
                n *= d
            o += -(-n // 32) * 32
        x, raw, ring, cf, cr, par = (fixed[k] for k in ("x", "raw", "ring", "cf", "cr", "par"))
        modc, gains, cond, one = (fixed[k] for k in ("modc", "gains", "cond", "one"))
        ident, mean_of, tri_le, tri_gt = (cf[:, i, :] for i in range(4))
        ident_r, neg_suffix, neg_ones, mask_sb, mask_ssd = (cr[:, i, :] for i in range(5))
        H = o
        R = H + 32768
        K = 1024
        h = at("h", [P, 2, KT, SEQ], F32R, H)

        def scratch(tag, base):
            return dict(rstd=at("rstd" + tag, [P, SEQ], F32, base), sq=at("sq" + tag, [P, 2, SEQ], F32, base + 2 * K),
                        hm=at("hm" + tag, [P, 2, SEQ], F32, base + 6 * K),
                        ssum=at("ssum" + tag, [P, SEQ], F32, base + 10 * K))

        s_low, s_high = scratch("_low", R), scratch("_high", R + 88 * K)

        qk0 = at("qk0", [P, 8, SEQ], F32, R)
        v0 = at("v0", [P, NT, SEQ], F32, R + 16 * K)
        zs = at("zs", [P, 8, SEQ], F32, R + 24 * K)
        xs = at("xs", [P, 16, SEQ], F32, R + 40 * K)
        ada_in0 = at("ada_in0", [P, 2, KT, ADA_W], F32, R + 72 * K)
        ada_acc0 = at("ada_acc0", [P, 2, ADA_W], F32, R + 88 * K)
        ub0 = at("ub0", [P, 4, UB], F32, R + 90 * K)
        cacc0 = at("cacc0", [P, 2, SEQ], F32, R + 90 * K + 4 * UB * 4 + 64)
        wdt_f = at("wdt_f", [P, KT, 16], F32, R + 103 * K - 512)
        sb_lr = at("sb_lr", [P, 2, 2, 1280], F32R, H)
        sb_l = at("sb_l", [P, 2, 1280], F32, H + 20 * K)
        sb_w = at("sb_w", [P, 2, 1280], F32, R + 88 * K)
        mix_sb = at("mix_sb", [P, 2, 4, SEQ], F32R, R + 72 * K)
        dts = at("dts", [P, 7, NT, 16], F32, R + 100 * K)
        dt_raw, dt_l, dt_v, dt_a, dt_acs, dt_w, a_neg_b = (dts[:, i] for i in range(7))
        acs = at("acs", [16, SEQ], F32, R + 98 * K)
        cb = at("cb", [P, SEQ], F32, H)
        xdt = at("xdt", [P, NT, 256], F32, H + 2 * K)
        xw = at("xw", [P, 3, 256], F32, H + 6 * K)
        b_tok = at("b_tok", [P, 3, P], F32, H + 9 * K)
        st = at("st", [P, 3, 256], F32, H + 11 * K)
        dm = at("dm", [P, 2, SEQ], F32, H + 14 * K)
        eb = at("eb", [P, 2, SEQ], F32, H + 18 * K)
        cs = at("cs", [P, 2, 384], F32, H + 22 * K)
        yt = at("yt", [P, SEQ], F32, H + 25 * K)
        mix_ssm = at("mix_ssm", [P, 2, 8, SEQ], F32R, R + 40 * K)
        wdt = at("wdt", [P, 2, KT, 16], F32R, R + 103 * K)
        y_h = at("y_h", [P, KT, SEQ], F32, H)
        oneh = at("oneh", [33, 640], F32, R + 24 * K)
        relt = at("relt", [33, 16], F32, R + 27 * K)
        table = at("table", [16, 640], F32, R + 28 * K)

        act = at("act", [P, 2, FT, SEQ], F32R, R)
        ub = at("ub", [P, 4, UB], F32, R + 88 * K)
        cg = at("cg", [P, 2, SEQ], F32, R + 88 * K + 4 * UB * 4 + 64)
        cv = at("cv", [P, SEQ], F32, R + 92 * K + 4 * UB * 4 + 64)
        ada_in1 = at("ada_in1", [P, 2, KT, ADA_W], F32, H + 16 * K)
        ada_acc1 = at("ada_acc1", [P, 2, ADA_W], F32, R + 100 * K)

        f1 = at("f1", [P, 16, SEQ], F32, R)
        v1 = at("v1", [P, NT, SEQ], F32, R + 32 * K)
        kcs = at("kcs", [P, 4, SEQ], F32, R + 40 * K)
        fl_r = at("fl_r", [P, 2, 16, 124], F32R, R + 48 * K)
        fl = at("fl", [P, 16, 124], F32, R + 64 * K)
        hid = at("hid", [P, 2, 124], F32, R + 72 * K)
        kcmp = at("kcmp", [P, 124], F32, R + 73 * K)
        vcmp = at("vcmp", [31, 256], F32, R + 74 * K)
        gates = at("gates", [P, 48, NT], F32, R + 75 * K)
        npar = at("npar", [P, NN], F32, R + 76 * K)
        wg_r = at("wg_r", [P, 2, KT, 48], F32R, R + 80 * K)
        s_p = at("s_p", [P, 3, 1280], F32, R + 40 * K)
        p_t = at("p_t", [P, 2, 1280], F32, R + 55 * K)
        q_st = at("q_st", [P, 2, SEQ], F32, R + 65 * K)
        u_b = at("u_b", [P, 2, 2, SEQ], F32, R + 84 * K)
        mx = at("mx", [P, 3, NT], F32, R + 92 * K)
        rs = at("rs", [P, 3, NT], F32, R + 92 * K + 64)
        sc = at("sc", [P, 3, NT], F32, R + 92 * K + 128)
        mix1 = at("mix1", [P, 2, KT, SEQ], F32R, H)
        y_r = at("y_r", [P, KT, SEQ], F32, R + 16 * K)
        assert top[0] <= nc.sbuf_usable_end, (top[0], nc.sbuf_usable_end)

        ps = ctx.enter_context(nc.psum_tensor("ps", [P, 8, SEQ], F32))
        table_d = nc.dram_tensor("rel_table", (16, P, 640), F32)

        def sem(name):
            return ctx.enter_context(nc.semaphore(name))

        const_in, x_in, ada_small, table_in = sem("const_in"), sem("x_in"), sem("ada_small"), sem("table_in")
        landed = [sem("w_landed0"), sem("w_landed1")]
        w_hi, w_lo, pe_done, evac = sem("w_hi"), sem("w_lo"), sem("pe_done"), sem("evac")
        ada_landed = [sem("ada_landed0"), sem("ada_landed1")]
        ada_sum, ada_mm, mod_ready = sem("ada_sum"), sem("ada_mm"), sem("mod_ready")
        cond_ready = sem("cond_ready")
        setup, table_mm, table_out, table_st = sem("setup"), sem("table_mm"), sem("table_out"), sem("table_st")
        n_sq, n_ss, n_rs, n_dv, n_hi, n_lo = (sem(k) for k in ("n_sq", "n_ss", "n_rs", "n_dv", "n_hi", "n_lo"))
        y_sq, y_sum, res = sem("y_sq"), sem("y_sum"), sem("res")
        pad, conv, silu_x = sem("pad"), sem("conv"), sem("silu_x")
        dt_mm, dt_dv, dt_ac, dt_tr, dt_col = (sem(k) for k in ("dt_mm", "dt_dv", "dt_ac", "dt_tr", "dt_col"))
        sb_z, sb_abs, sb_e, sb_L, sb_hi, sb_lo, sb_s, sb_wt, sb_pv, sb_mix = (
            sem(k) for k in ("sb_z", "sb_abs", "sb_e", "sb_L", "sb_hi", "sb_lo", "sb_s", "sb_wt", "sb_pv", "sb_mix"))
        g_pe, g_ac, g_dv = sem("g_pe"), sem("g_ac"), sem("g_dv")
        hd_bc, hd_e, hd_mask, hd_d, hd_x, hd_dv, hd_y = (
            sem(k) for k in ("hd_bc", "hd_e", "hd_mask", "hd_d", "hd_x", "hd_dv", "hd_y"))
        yg, ms_sq, ms_dv, ms_lo = sem("yg"), sem("ms_sq"), sem("ms_dv"), sem("ms_lo")
        f_dv, f_gelu = sem("f_dv"), sem("f_gelu")
        gt_w, gt_mm, gt_ac, gt_dv = sem("gt_w"), sem("gt_mm"), sem("gt_ac"), sem("gt_dv")
        npar_in, shift_in, fl_dv, fl_hi, fl_lo, c_hid, c_mm, c_out = (
            sem(k) for k in ("npar_in", "shift_in", "fl_dv", "fl_hi", "fl_lo", "c_hid", "c_mm", "c_out"))
        u_in = [sem("u_in0"), sem("u_in1")]
        a_q, a_s, a_mx, a_neg, a_p, a_sc, a_n, a_t, a_pt, a_pv, a_mix = (
            sem(k) for k in ("a_q", "a_s", "a_mx", "a_neg", "a_p", "a_sc", "a_n", "a_t", "a_pt", "a_pv", "a_mix"))
        out_done = sem("out_done")

        def pc(name, i, rows=P):
            return par[0:rows, bass.ds(pcol[name][0] + i, 1)]

        def wait(e, s, value):
            if not isinstance(value, int) or value > 0:
                e.wait_ge(s, value)

        def product3(e, out, a, b, first, last):
            for n, (i, j) in enumerate(((0, 0), (0, 1), (1, 0))):
                mm = e.matmul(out, a[i], b[j], start=first and n == 0, stop=last and n == 2)
            return mm

        def a_col(i, k):
            return gains[:, 16 * i + k:16 * i + k + 1]

        def shift_col(i, k):
            c = 48 * (i // 2) + 24 * (i % 2) + k
            return modc[:, c:c + 1]

        def g_col(i, k):
            return gains[:, 16 * i + 8 + k:16 * i + 9 + k]

        norms = [s_low, s_low, s_high, s_low]
        posts = [s_low, s_high, s_low, s_high]
        ys = [y_h, y_h, y_r, y_h]
        RS_IN, RS_SSM, RS_OUT = [0, 6, 10, 14], 2, [4, 8, 12, 16]
        SS_IN, SS_SSM, SS_OUT = [0, 10, 19, 28], 8, [9, 18, 27, 36]
        SQ_IN = [0, 8, 16, 24]

        T_BEFORE = [14 * (u // 6) + 7 * (u // 3 % 2) + 3 * (u % 3) for u in range(13)]

        def nsa_rows(u):
            if u % 3 < 2:
                return [(qt, (QOFF[qt], P * (qt + 1))) for qt in (3, 0, 2, 1)]
            return [(qt, (7 * qt + 4 * qt * (qt - 1), 7 + 8 * qt)) for qt in range(NT)]

        block = ctx.enter_context(nc.Block())

        @block.sync
        def _(sp):
            def load(name, i, s):
                ph = plan[name]
                src, first = weights[name]
                c = ph["c0"] + i
                wait(sp, w_lo, c - 1)
                sp.dma_start(raw[:, s, 0:ph["size"] * P], src[first + i]).then_inc(landed[s], 16)

            def load_ada(a, s, buf):
                wait(sp, ada_sum, 8 * (a - 1))
                sp.dma_start(buf[:, s], ada[a]).then_inc(ada_landed[s], 16)

            sp.dma_start(par[:, :], params).then_inc(const_in, 16)
            sp.dma_start(cf[:, :, :], consts[:, 0:4]).then_inc(const_in, 16)
            sp.dma_start(dm[:, 0:2, :].rearrange("p a b -> p (a b)")[:, 0:5 * P],
                         consts[:, 4:9].rearrange("p a b -> p (a b)")).then_inc(const_in, 16)
            sp.dma_start(wdt_f[:, :, :], w_dt).then_inc(const_in, 16)
            sp.dma_start(oneh[:, :], onehot).then_inc(const_in, 16)
            sp.dma_start(relt[0:REL_BUCKETS, :], relb).then_inc(const_in, 16)
            load_ada(0, 0, ada_in0)
            load_ada(1, 1, ada_in0)
            sp.dma_start(x[:, :, :], x_t.rearrange("(k p) t -> p k t", p=P)).then_inc(x_in, 16)
            load_ada(2, 0, ada_in0)
            load_ada(3, 1, ada_in0)
            for a in range(4, ADA_FIRST):
                load_ada(a, a % 2, ada_in0)
            load("v0", 0, 0)
            load("v0", 1, 1)
            for name, ada_at in (("q", 8), ("k", 10), ("xbc", 12), ("z", 20)):
                n = plan[name]["n"] // 2
                if name == "z":
                    sp.wait_ge(table_out, 2)
                    sp.dma_start(table_d.ap(),
                                 table[:, :].unsqueeze(1).to_broadcast([16, P, 640])).then_inc(table_st, 16)
                with sp.Fori(0, n) as t:
                    for s in range(2):
                        load(name, 2 * t + s, s)
                        load_ada(2 * t + (ada_at + s), s, ada_in0)
            with sp.Fori(0, 4) as t:
                for s in range(2):
                    load("out0", 2 * t + s, s)
            with sp.Fori(0, 11) as t:
                for s in range(2):
                    load("up0", 2 * t + s, s)
            def down_loads(t):
                for i in range(4):
                    load("down0", 4 * t + i, i % 2)
                    load_ada(6 * t + (24 + i), i % 2, ada_in1)
                for i in range(2):
                    load_ada(6 * t + (28 + i), i % 2, ada_in1)

            sp.wait_ge(pe_done, plan["down0"]["ev0"])
            with sp.Fori(0, 4) as t:
                down_loads(t)
            load("v1", 0, 0)
            load("v1", 1, 1)
            wait(sp, n_hi, SQ_IN[2] + 8)
            sp.dma_start(npar[:, :], nsa_params).then_inc(npar_in, 16)
            with sp.Fori(0, 4) as t:
                for s in range(2):
                    load("f1", 2 * t + s, s)
            load("w1", 0, 0)
            load("w1", 1, 1)
            for kv in range(2):
                sp.wait_ge(evac, plan["w1"]["t0"])
                wait(sp, fl_dv, 16 * kv)
                for g in range(NSA_GROUPS):
                    rows = f1[HD * (g % 2):HD * (g % 2) + HD, 8 + 2 * kv + g // 2, :]
                    sp.dma_start(kcs[0:HD, g, :], rows).then_inc(shift_in, 16)
                    sp.dma_start(kcs[HD:P, g, 0:SEQ - 1], rows[:, 1:SEQ]).then_inc(shift_in, 16)
            load("w1", 2, 0)
            load("w1", 3, 1)
            load("out1", 0, 0)
            load("out1", 1, 1)
            sp.wait_ge(table_st, 16)
            sp.wait_ge(c_out, 2)
            for pair in range(8):
                wait(sp, a_mx, 24 * (pair - 1))
                head = 8 * (pair // 4) + pair % 4
                src = bass.AP(table_d, head * P * 640 + P - 1, [[640 - 1, P], [4 * P * 640, 2], [1, SEQ]])
                sp.dma_start(u_b[:, pair % 2], src).then_inc(u_in[pair % 2], 16)
            load("out1", 2, 0)
            load("out1", 3, 1)
            with sp.Fori(0, 11) as t:
                for s in range(2):
                    load("up1", 2 * t + s, s)
            with sp.Fori(0, 8) as t:
                for s in range(2):
                    load("down1", 2 * t + s, s)
            for k in range(KT):
                sp.wait_ge(res, 48 + 2 * k + 2)
                sp.dma_start(out_t[k * P:(k + 1) * P, :], x[:, k, :]).then_inc(out_done, 16)
            sp.wait_ge(out_done, 16 * KT)

        @block.scalar
        def _(sa):
            def round_next(name, i, s):
                ph = plan[name]
                n = ph["size"] * P
                nth = ph["c0"] // 2 + (1 if s == 0 else 2)
                o_ = 1 - s
                sa.wait_ge(landed[o_], 16 * nth + (16 // 2) * (i - s))
                sa.wait_ge(pe_done, ph["ev0"] + ph["per"] * i)
                sa.activation(ring[:, o_, 0, 0:n], raw[:, o_, 0:n], ACT.Copy).then_inc(w_hi, 1)

            def round_chunk(c, lo=0):
                sa.wait_ge(landed[c % 2], 16 * (c // 2 + 1))
                sa.activation(ring[:, c % 2, 0, lo:CW], raw[:, c % 2, lo:CW], ACT.Copy).then_inc(w_hi, 1)

            def root(base, sums, s):
                sa.wait_ge(n_ss, sums)
                sa.activation(s["rstd"][:, :], ps[:, 6, :], ACT.Ln, bias=EPS).then_inc(n_rs, 1)
                sa.wait_ge(n_rs, base + 1)
                sa.activation(s["rstd"][:, :], s["rstd"][:, :], ACT.Exp, scale=-0.5).then_inc(n_rs, 1)

            def norm_in(i):
                s = norms[i]
                for k in range(KT):
                    if i == 0:
                        sa.wait_ge(x_in, 16)
                    else:
                        sa.wait_ge(res, 16 * (i - 1) + 2 * k + 2)
                    if k >= 2:
                        sa.wait_ge(n_ss, SS_IN[i] + k - 1)
                    sa.activation(s["sq"][:, k % 2], x[:, k], ACT.Square).then_inc(n_sq, 1)
                root(RS_IN[i], SS_IN[i] + KT, s)
                for k in range(KT):
                    sa.wait_ge(n_dv, 16 * i + 2 * k + 2)
                    sa.activation(h[:, 0, k], s["hm"][:, k % 2], ACT.Copy).then_inc(n_hi, 1)

            def evac_tile(name, x_, bank, out, func=ACT.Copy, **kw):
                sa.wait_ge(pe_done, plan[name]["ev0"] + 1 + x_)
                sa.activation(out, ps[:, bank, :], func, **kw).then_inc(evac, 1)

            def plain(name, out, first, func=ACT.Copy, **kw):
                with sa.Fori(0, plan[name]["n"] // 2) as t:
                    for s in range(2):
                        round_next(name, 2 * t + s, s)
                        for half in range(2):
                            x_ = 4 * t + (2 * s + half)
                            evac_tile(name, x_, 2 * s + half, out[:, bass.ds(x_ + first, 1), :], func, **kw)

            def tokens(name, i, v):
                ph = plan[name]
                c = ph["c0"]
                sa.wait_ge(pe_done, ph["ev0"] + 1)
                round_chunk(c + 2)
                for t in range(NT):
                    sa.wait_ge(pe_done, ph["ev0"] + 2 + t)
                    sa.activation(v[:, t], ps[:, t, :], ACT.Copy).then_inc(evac, 1)

            def y_tile(p, name, x_, done, bank, par_):
                s = posts[p]
                sa.wait_ge(pe_done, done)
                sa.activation(ys[p][:, bass.ds(x_, 1), :], ps[:, bank:bank + 1, :], ACT.Copy).then_inc(y_sq, 1)
                wait(sa, y_sum, 9 * p + x_)
                sa.activation(s["sq"][:, par_], ps[:, bank, :], ACT.Square).then_inc(evac, 1)

            def root_out(p):
                root(RS_OUT[p], SS_OUT[p] + 1, posts[p])

            def ffn_up(l):
                name = f"up{l}"
                with sa.Fori(0, FT // 2) as t:
                    for s in range(2):
                        round_next(name, 2 * t + s, s)
                        evac_tile(name, 4 * t + 2 * s, 2 * s, ub[:, 2 * s, PAD:])
                        sa.wait_ge(f_dv, 18 * t + (9 * FT * l + 9 * s + 3))
                        sa.activation(cg[:, s], cg[:, s], ACT.Gelu_apprx_tanh).then_inc(f_gelu, 1)
                        evac_tile(name, 4 * t + (2 * s + 1), 2 * s + 1, ub[:, 2 * s + 1, PAD:])

            def ffn_down(l):
                name = f"down{l}"
                ph = plan[name]

                def body(t, last=False):
                    for i in range(4):
                        if not (last and i == 3):
                            round_next4(name, t, i)
                        if i % 2:
                            y_tile(1 + 2 * l, name, 2 * t + i // 2, 4 * t + (ph["ev0"] + i + 1), i // 2, i // 2)

                def round_next4(name, t, i):
                    n = ph["size"] * P
                    o_ = (i + 1) % 2
                    c = ph["c0"] + i + 1
                    sa.wait_ge(landed[o_], 32 * t + 16 * (c // 2 + 1))
                    sa.wait_ge(pe_done, 4 * t + (ph["ev0"] + i))
                    sa.activation(ring[:, o_, 0, 0:n], raw[:, o_, 0:n], ACT.Copy).then_inc(w_hi, 1)

                if l == 0:
                    with sa.Fori(0, 4) as t:
                        body(t)
                    round_chunk(plan["v1"]["c0"], 11 * P)
                else:
                    with sa.Fori(0, 3) as t:
                        body(t)
                    body(3, last=True)

            sa.wait_ge(const_in, 96)
            sa.activation(cond[:, :], par[:, pcol["cond"][0]:pcol["cond"][0] + KT], ACT.Silu).then_inc(cond_ready, 1)
            round_chunk(0)
            round_chunk(1)
            norm_in(0)
            tokens("v0", 0, v0)
            plain("q", qk0, 0, scale=HD ** -0.5)
            plain("k", qk0, 4)
            with sa.Fori(0, 4) as t:
                for s in range(2):
                    round_next("xbc", 2 * t + s, s)
                    for half in range(2):
                        x_ = 4 * t + (2 * s + half)
                        evac_tile("xbc", x_, 2 * s + half, ub0[:, 2 * s + half, PAD:])
                        sa.wait_ge(conv, 16 * t + (4 * (2 * s + half) + 4))
                        sa.activation(xs[:, bass.ds(x_, 1), :], cacc0[:, half:half + 1, :], ACT.Silu).then_inc(silu_x, 1)
            sa.wait_ge(table_st, 16)
            plain("z", zs, 0, ACT.Silu)

            sa.activation(dts[:, 6, 0, :], par[:, pcol["a_log"][0]:pcol["a_log"][0] + 16], ACT.Exp).then_inc(dt_ac, 1)
            sa.wait_ge(dt_dv, 2)
            sa.activation(dt_l, dt_l, ACT.Exp).then_inc(dt_ac, 1)
            sa.wait_ge(dt_ac, 2)
            sa.activation(dt_l, dt_l, ACT.Ln, bias=1.0).then_inc(dt_ac, 1)
            sa.wait_ge(dt_mm, 3)
            sa.wait_ge(dt_dv, 6)
            sa.activation(dt_w, ps[:, 7, 64:128].rearrange("p (t h) -> p t h", t=NT), ACT.Exp).then_inc(dt_ac, 1)

            def softplus(u):
                if u >= 2:
                    sa.wait_ge(sb_lo, u - 1)
                for n, (at_, w) in enumerate(BANKS):
                    sa.wait_ge(sb_z, 3 * u + n + 1)
                    sa.activation(sb_l[:, u % 2, at_:at_ + w], ps[:, 3 * (u % 2) + n, 0:w], ACT.Abs).then_inc(sb_abs, 1)
                sa.wait_ge(sb_abs, 3 * u + 3)
                sa.activation(sb_l[:, u % 2], sb_l[:, u % 2], ACT.Exp, scale=-1.0).then_inc(sb_e, 1)
                sa.wait_ge(sb_e, 2 * u + 1)
                sa.activation(sb_l[:, u % 2], sb_l[:, u % 2], ACT.Ln, bias=1.0).then_inc(sb_e, 1)

            softplus(0)
            softplus(1)
            for u in range(SB_HEADS):
                wait(sa, sb_pv, u - 1)
                for n, (at_, w) in enumerate(BANKS):
                    sa.wait_ge(sb_s, 3 * u + n + 1)
                    sa.activation(sb_w[:, u % 2, at_:at_ + w], ps[:, 3 * (u % 2) + n, 0:w], ACT.Exp).then_inc(sb_wt, 1)
                if u + 2 < SB_HEADS:
                    softplus(u + 2)

            def gated_squares(k):
                sa.wait_ge(yg, 3 * k + 2)
                sa.activation(s_low["sq"][:, k % 2], zs[:, k], ACT.Square).then_inc(ms_sq, 1)

            for g in range(SSM_GROUPS):
                wait(sa, hd_dv, 16 * g)
                wait(sa, hd_y, 4 * g)
                sa.wait_ge(g_pe, 5 * g + 1)
                sa.activation(cb[:, :], ps[:, 0, :], ACT.Copy).then_inc(g_ac, 1)
                sa.wait_ge(g_pe, 5 * g + 4)
                sa.activation(b_tok[:, :, :], ps[:, 3, 0:384].rearrange("p (c n) -> p c n", c=3), ACT.Copy).then_inc(g_ac, 1)
                sa.wait_ge(g_pe, 5 * g + 5)
                sa.activation(st[:, 0, :], ps[:, 4, 0:256], ACT.Copy).then_inc(g_ac, 1)
                for hh in range(4):
                    n = 4 * g + hh
                    sa.wait_ge(hd_bc, n + 1)
                    if n >= 2:
                        sa.wait_ge(hd_dv, 4 * (n - 1))
                    sa.activation(eb[:, n % 2], ps[:, 6 + n % 2, :], ACT.Exp).then_inc(hd_e, 1)
                    if hh == 2:
                        gated_squares(2 * g)
                    sa.wait_ge(hd_d, n + 1)
                    sa.activation(dm[:, n % 2], dm[:, n % 2], ACT.Exp).then_inc(hd_x, 1)
                gated_squares(2 * g + 1)
            root(RS_SSM, SS_SSM + 1, s_low)

            with sa.Fori(0, 4) as t:
                for s in range(2):
                    round_next("out0", 2 * t + s, s)
                    y_tile(0, "out0", 2 * t + s, 2 * t + (plan["out0"]["ev0"] + s + 1), s, s)
            round_chunk(plan["up0"]["c0"], 12 * P)
            root_out(0)
            norm_in(1)
            ffn_up(0)
            ffn_down(0)
            root_out(1)

            sa.wait_ge(pe_done, plan["v1"]["ev0"])
            round_chunk(plan["v1"]["c0"] + 1)
            norm_in(2)
            tokens("v1", 2, v1)
            with sa.Fori(0, 2) as t:
                for s in range(2):
                    round_next("f1", 2 * t + s, s)
                    for half in range(2):
                        x_ = 4 * t + (2 * s + half)
                        evac_tile("f1", x_, 2 * s + half, f1[:, bass.ds(x_, 1), :], scale=HD ** -0.5)
            with sa.Fori(2, 4) as t:
                for s in range(2):
                    round_next("f1", 2 * t + s, s)
                    for half in range(2):
                        x_ = 4 * t + (2 * s + half)
                        evac_tile("f1", x_, 2 * s + half, f1[:, bass.ds(x_, 1), :])
            for kv in range(2):
                sa.wait_ge(fl_dv, 16 * kv + 16)
                wait(sa, pe_done, plan["w1"]["ev0"] + 2 * kv)
                sa.activation(fl_r[:, 0], fl[:, :, :], ACT.Copy).then_inc(fl_hi, 1)
                for part in range(2):
                    round_next("w1", 2 * kv + part, part)
                sa.wait_ge(pe_done, plan["w1"]["ev0"] + 2 * kv + 2)
                for hh in range(2):
                    col = ncol["b1"][0] + 2 * kv + hh
                    wait(sa, c_mm, kv)
                    sa.activation(hid[:, hh], ps[:, 2 * kv + hh, 0:124], ACT.Silu,
                                  bias=npar[:, col:col + 1]).then_inc(evac, 1)
            sa.wait_ge(gt_mm, 1)
            sa.activation(gates[:, :, :].rearrange("p c t -> p t c"),
                          ps[:, 6, 0:192].rearrange("p (t c) -> p t c", t=NT), ACT.Exp, scale=-1.0).then_inc(gt_ac, 1)

            def nsa_exp(gp, t, u):
                r = u % 3
                sa.wait_ge(a_neg, 12 * t + (24 * gp + u + 1))
                for qt, (at_, w) in nsa_rows(u):
                    sa.activation(s_p[:, r, at_:at_ + w], s_p[:, r, at_:at_ + w], ACT.Exp,
                                  bias=mx[:, r, qt:qt + 1], accum_out=rs[:, r, qt:qt + 1]).then_inc(a_p, 1)

            def nsa_take(gp, t, u):
                sa.wait_ge(a_pv, 12 * t + (24 * gp + max(0, u - 1)))
                for n, (at_, w) in enumerate(BANKS[:3 if u % 3 < 2 else 1]):
                    rows = P if u % 3 < 2 else CMP_N
                    sa.wait_ge(a_t, 28 * t + (56 * gp + T_BEFORE[u] + n + 1))
                    sa.activation(p_t[0:rows, u % 2, at_:at_ + w], ps[0:rows, 3 + n, 0:w], ACT.Copy).then_inc(a_pt, 1)

            for gp in range(2):
                with sa.Fori(0, 2) as t:
                    for v in range(15):
                        if v < 12:
                            nsa_exp(gp, t, v)
                        if 2 <= v < 14:
                            nsa_take(gp, t, v - 2)
            with sa.Fori(0, 2) as t:
                for s in range(2):
                    round_next("out1", 2 * t + s, s)
                    for half in range(2):
                        x_ = 4 * t + (2 * s + half)
                        y_tile(2, "out1", x_, 4 * t + (plan["out1"]["ev0"] + 2 * s + half + 1), 2 * s + half, half)
            root_out(2)
            norm_in(3)
            ffn_up(1)
            ffn_down(1)
            root_out(3)

        @block.gpsimd
        def _(gp_):
            def lower(name):
                ph = plan[name]
                n = ph["size"] * P

                def body(i, s):
                    gp_.wait_ge(w_hi, i + (ph["c0"] + 1 + ph["extra"]))
                    gp_.tensor_tensor(ring[:, s, 1, 0:n], raw[:, s, 0:n], ring[:, s, 0, 0:n].bitcast(F32),
                                      ALU.subtract).then_inc(w_lo, 1)
                if name in ("v0", "v1"):
                    body(0, 0)
                    body(1, 1)
                    return
                with gp_.Fori(0, ph["n"] // 2) as t:
                    for s in range(2):
                        body(2 * t + s, s)

            def norm_in(i):
                s = norms[i]
                for k in range(KT):
                    gp_.wait_ge(n_hi, SQ_IN[i] + k + 1)
                    gp_.tensor_tensor(h[:, 1, k], s["hm"][:, k % 2], h[:, 0, k].bitcast(F32),
                                      ALU.subtract).then_inc(n_lo, 1)

            lower("v0")
            norm_in(0)
            for name in ("q", "k", "xbc", "z"):
                lower(name)
            for u in range(SB_HEADS):
                gp_.wait_ge(sb_hi, u + 1)
                gp_.tensor_tensor(sb_lr[:, u % 2, 1], sb_l[:, u % 2], sb_lr[:, u % 2, 0].bitcast(F32),
                                  ALU.subtract).then_inc(sb_lo, 1)
            for k in range(8):
                gp_.wait_ge(ms_dv, 2 * k + 2)
                gp_.tensor_tensor(mix_ssm[:, 1, k], s_low["hm"][:, k % 2], mix_ssm[:, 0, k].bitcast(F32),
                                  ALU.subtract).then_inc(ms_lo, 1)
            lower("out0")
            norm_in(1)
            lower("up0")
            lower("down0")
            norm_in(2)
            lower("v1")
            lower("f1")
            for kv in range(2):
                gp_.wait_ge(fl_hi, kv + 1)
                gp_.tensor_tensor(fl_r[:, 1], fl[:, :, :], fl_r[:, 0].bitcast(F32), ALU.subtract).then_inc(fl_lo, 1)
                for part in range(2):
                    c = plan["w1"]["c0"] + 2 * kv + part
                    gp_.wait_ge(w_hi, c + 1 + plan["w1"]["extra"])
                    gp_.tensor_tensor(ring[:, part, 1], raw[:, part], ring[:, part, 0].bitcast(F32),
                                      ALU.subtract).then_inc(w_lo, 1)
            lower("out1")
            norm_in(3)
            lower("up1")
            lower("down1")

        @block.tensor
        def _(pe):
            def weights_of(s, j):
                return ring[:, s, 0, j * P:(j + 1) * P], ring[:, s, 1, j * P:(j + 1) * P]

            def split(tensor, k):
                return tensor[:, 0, k], tensor[:, 1, k]

            def norm_sums(i):
                wait(pe, n_rs, RS_IN[i])
                for k in range(KT):
                    pe.wait_ge(n_sq, SQ_IN[i] + k + 1)
                    pe.matmul(ps[:, 6, :], mean_of, norms[i]["sq"][:, k % 2], start=k == 0, stop=k == KT - 1).then_inc(n_ss, 1)

            def out_sums(p):
                pe.wait_ge(y_sum, 9 * p + 9)
                pe.matmul(ps[:, 6, :], mean_of, posts[p]["ssum"][:, :], start=True, stop=True).then_inc(n_ss, 1)

            def tokens(name, i):
                ph = plan[name]
                wait(pe, evac, ph["t0"])
                for part in range(2):
                    pe.wait_ge(w_lo, ph["c0"] + part + 1)
                    for n in range(16):
                        k, t = (n // 4, n % 4) if part == 0 else (n % 4, n // 4)
                        kk = 4 * part + k
                        if n < 4 if part else n % 4 == 0:
                            pe.wait_ge(n_lo, 8 * i + kk + 1)
                        hs = tuple(a[:, t * P:(t + 1) * P] for a in split(h, kk))
                        w = tuple(ring[:, part, j, k * SEQ:(k + 1) * SEQ] for j in range(2))
                        mm = product3(pe, ps[:, t, :], hs, w, kk == 0, kk == KT - 1)
                        if (part == 0 and n == 15) or (part == 1 and k == 3):
                            mm.then_inc(pe_done, 1)

            def features(name, i, s, rhs, banks=(0, 1, 2, 3), free=3):
                ph = plan[name]
                pe.wait_ge(w_lo, i + (ph["c0"] + 1))
                for half in range(2):
                    pe.wait_ge(evac, 2 * i + (ph["t0"] + half - free))
                    for k in range(KT):
                        mm = product3(pe, ps[:, banks[2 * s + half], :], weights_of(s, 8 * half + k), split(rhs, k),
                                      k == 0, k == KT - 1)
                    mm.then_inc(pe_done, 1)

            def ada_sum_up(a, s, acc):
                pe.wait_ge(ada_sum, 8 * a + 8)
                for half in range(2):
                    mm = pe.matmul(ps[:, 7, bass.ds(2 * a + half, 1)], acc[:, s, half * P:(half + 1) * P], one[:, :],
                                   start=True, stop=True)
                mm.then_inc(ada_mm, 1)

            def feature_phase(name, ada_at=None):
                with pe.Fori(0, plan[name]["n"] // 2) as t:
                    for s in range(2):
                        features(name, 2 * t + s, s, h)
                        if ada_at is not None:
                            ada_sum_up(2 * t + (ada_at + s), s, ada_acc0)

            pe.wait_ge(const_in, 96)
            pe.wait_ge(setup, 2)
            for n in range(2):
                pe.matmul(ps[0:16, n, 0:320], relt[:, :], oneh[:, 320 * n:320 * n + 320],
                          start=True, stop=True).then_inc(table_mm, 1)
            for a in range(ADA_FIRST):
                ada_sum_up(a, a % 2, ada_acc0)
            norm_sums(0)
            pe.wait_ge(table_out, 2)
            tokens("v0", 0)
            feature_phase("q", 8)
            feature_phase("k", 10)
            feature_phase("xbc", 12)
            feature_phase("z", 20)

            pe.wait_ge(setup, 5)
            for t in range(NT):
                for k in range(KT):
                    hs = tuple(a[:, t * P:(t + 1) * P] for a in split(h, k))
                    mm = product3(pe, ps[:, 6, 16 * t:16 * t + 16], hs, split(wdt, k), k == 0, k == KT - 1)
            mm.then_inc(dt_mm, 1)

            def sb_scores(u):
                b, i, bank = u % 2, u // 2, 3 * (u % 2)
                if u < 2:
                    pe.wait_ge(evac, plan["out0"]["t0"])
                else:
                    pe.wait_ge(sb_wt, 3 * (u - 1))
                rows = slice(HD * b, HD * b + HD)
                for n, tiles in enumerate(((0,), (1, 3), (2,))):
                    for kt in tiles:
                        off = KOFF[kt] - SEQ * n
                        mm = pe.matmul(ps[:, bank + n, off:off + SEQ - P * kt], qk0[rows, 4 + i, P * kt:P * kt + P],
                                       qk0[rows, i, P * kt:], start=kt == tiles[0], stop=False, skip_group_check=True)
                        mm = pe.matmul(ps[:, bank + n, off:off + P], ident_r, mask_sb,
                                       start=False, stop=False, skip_group_check=True)
                    mm.then_inc(sb_z, 1)

            def sb_suffix(u):
                bank = 3 * (u % 2)
                pe.wait_ge(sb_lo, u + 1)
                for n, tiles in enumerate(((0,), (1, 3), (2,))):
                    for kt in tiles:
                        for k2 in range(kt, NT):
                            w = SEQ - P * k2
                            off = KOFF[kt] - SEQ * n + P * (k2 - kt)
                            for part in range(2):
                                mm = pe.matmul(ps[:, bank + n, off:off + w], neg_suffix if k2 == kt else neg_ones,
                                               sb_lr[:, u % 2, part, KOFF[k2]:KOFF[k2] + w], start=False,
                                               stop=False, skip_group_check=True)
                    mm.then_inc(sb_s, 1)

            def sb_values(u):
                b, i = u % 2, u // 2
                pe.wait_ge(sb_wt, 3 * u + 3)
                if u % 2 == 0 and u >= 4:
                    pe.wait_ge(sb_mix, 2 * (i - 1))
                for kt in range(NT):
                    mm = pe.matmul(ps[HD * b:HD * b + HD, 6 + i % 2, P * kt:], v0[:, kt, HD * u:HD * u + HD],
                                   sb_w[:, u % 2, KOFF[kt]:KOFF[kt] + SEQ - P * kt], start=kt == 0, stop=kt == NT - 1,
                                   skip_group_check=True)
                mm.then_inc(sb_pv, 1)

            sb_scores(0)
            pe.wait_ge(dt_dv, 5)
            pe.wait_ge(mod_ready, 3)
            for n, tri in enumerate((tri_le, tri_gt)):
                pe.matmul(ps[:, 7, 64 * n:64 * n + 64], tri, dt_a.rearrange("p t h -> p (t h)"),
                          start=True, stop=True).then_inc(dt_mm, 1)
            sb_scores(1)
            pe.wait_ge(dt_dv, 6)
            for t in range(NT):
                mm = pe.transpose(ps[0:16, 6, P * t:P * t + P], dt_acs[:, t, :], ident)
            mm.then_inc(dt_tr, 1)
            pe.wait_ge(dt_dv, 8)
            for u in range(SB_HEADS):
                sb_suffix(u)
                if u >= 1:
                    sb_values(u - 1)
                if u + 2 < SB_HEADS:
                    sb_scores(u + 2)
            sb_values(SB_HEADS - 1)

            for g in range(SSM_GROUPS):
                if g == 0:
                    pe.wait_ge(sb_mix, 8)
                else:
                    pe.wait_ge(g_ac, 3 * g)
                    pe.wait_ge(yg, 6 * g - 2)
                for c in range(NT):
                    mm = pe.matmul(ps[:, 0, P * c:P * c + P], xs[:, 8 + g, P * c:P * c + P], xs[:, 12 + g, P * c:P * c + P],
                                   start=True, stop=True)
                mm.then_inc(g_pe, 1)
                for n in range(2):
                    for j in range(2):
                        for f in range(2):
                            c = 2 * n + j
                            mm = pe.transpose(ps[:, 1 + n, 256 * j + P * f:256 * j + P * f + P],
                                              xs[:, 2 * g + f, P * c:P * c + P], ident)
                    mm.then_inc(g_pe, 1)
                for c in range(3):
                    mm = pe.transpose(ps[:, 3, P * c:P * c + P], xs[:, 8 + g, P * c:P * c + P], ident)
                mm.then_inc(g_pe, 1)
                pe.wait_ge(g_ac, 3 * g + 2)
                pe.wait_ge(g_dv, 4 * g + 4)
                wait(pe, hd_dv, 16 * g)
                for c in range(3):
                    mm = pe.matmul(ps[:, 4 + c // 2, 256 * (c % 2):256 * (c % 2) + 256], b_tok[:, c], xw[:, c],
                                   start=True, stop=True)
                mm.then_inc(g_pe, 1)

                def head_y(n):
                    hh = n % 4
                    b = hh % 2
                    pe.wait_ge(hd_dv, 4 * n + 4)
                    out = ps[HD * b:HD * b + HD, 1 + hh // 2, :]
                    for c in range(NT):
                        mm = pe.matmul(out[:, P * c:P * c + P], xdt[:, c, HD * hh:HD * hh + HD],
                                       dm[:, n % 2, P * c:P * c + P], start=c == 0, stop=False, skip_group_check=True)
                    for c in range(1, NT):
                        mm = pe.matmul(out[:, P * c:P * c + P], st[:, c - 1, HD * hh:HD * hh + HD],
                                       cs[:, n % 2, P * (c - 1):P * c], start=False, stop=c == NT - 1,
                                       skip_group_check=True)
                    mm.then_inc(hd_y, 1)

                for hh in range(4):
                    n = 4 * g + hh
                    bank = 6 + n % 2
                    if n >= 2:
                        pe.wait_ge(hd_d, n - 1)
                    pe.matmul(ps[:, bank, :], ident[0:16, n:n + 1].to_broadcast([16, P]), acs[:, :],
                              start=True, stop=False, skip_group_check=True).then_inc(hd_bc, 1)
                    pe.wait_ge(hd_e, n + 1)
                    pe.matmul(ps[:, bank, :].rearrange("p (c l) -> p c l", c=NT), ident_r,
                              mask_ssd.unsqueeze(1).to_broadcast([P, NT, P]), start=False, stop=True,
                              skip_group_check=True).then_inc(hd_mask, 1)
                    if hh:
                        head_y(n - 1)
                head_y(4 * g + 3)
            pe.wait_ge(yg, 24)
            pe.matmul(ps[:, 6, :], mean_of, s_low["ssum"][:, :], start=True, stop=True).then_inc(n_ss, 1)

            pe.wait_ge(ms_lo, 8)

            def mixed(k):
                return split(mix_sb, k) if k < 4 else split(mix_ssm, k - 4)

            with pe.Fori(0, 4) as t:
                for s in range(2):
                    ph = plan["out0"]
                    pe.wait_ge(w_lo, 2 * t + (ph["c0"] + s + 1))
                    pe.wait_ge(evac, 2 * t + (ph["t0"] + s - 1))
                    for k in range(12):
                        mm = product3(pe, ps[:, s, :], weights_of(s, k), mixed(k), k == 0, k == 11)
                    mm.then_inc(pe_done, 1)
            out_sums(0)

            def ffn(l):
                i = 1 + 2 * l
                norm_sums(i)
                pe.wait_ge(n_lo, 8 * i + 8)
                feature_phase(f"up{l}")
                ph = plan[f"down{l}"]
                pe.wait_ge(f_dv, 9 * FT * (l + 1))
                pe.wait_ge(evac, ph["t0"])
                with pe.Fori(0, 4) as t:
                    for c in range(4):
                        pe.wait_ge(w_lo, 4 * t + (ph["c0"] + c + 1))
                        if c % 2 == 0:
                            pe.wait_ge(evac, 2 * t + (ph["t0"] + c // 2 - 1))
                        for j in range(11):
                            k = 11 * (c % 2) + j
                            mm = product3(pe, ps[:, c // 2, :], weights_of(c % 2, j), split(act, k), k == 0, k == FT - 1)
                        mm.then_inc(pe_done, 1)
                        if l == 0:
                            ada_sum_up(6 * t + (24 + c), c % 2, ada_acc1)
                    if l == 0:
                        for c in range(2):
                            ada_sum_up(6 * t + (28 + c), c, ada_acc1)
                out_sums(1 + 2 * l)

            ffn(0)

            norm_sums(2)
            tokens("v1", 2)
            feature_phase("f1")
            pe.wait_ge(gt_w, 2)
            for t in range(NT):
                for k in range(KT):
                    hs = tuple(a[:, t * P:(t + 1) * P] for a in split(h, k))
                    mm = product3(pe, ps[:, 6, 48 * t:48 * t + 48], hs, split(wg_r, k), k == 0, k == KT - 1)
            mm.then_inc(gt_mm, 1)
            for kv in range(2):
                for part in range(2):
                    ph = plan["w1"]
                    pe.wait_ge(w_lo, ph["c0"] + 2 * kv + part + 1)
                    pe.wait_ge(fl_lo, kv + 1)
                    pe.wait_ge(evac, ph["t0"])
                    for i in range(8):
                        for hh in range(2):
                            mm = product3(pe, ps[:, 2 * kv + hh, 0:124], weights_of(part, 2 * i + hh),
                                          tuple(fl_r[:, j, 8 * part + i] for j in range(2)),
                                          part == 0 and i == 0, part == 1 and i == 7)
                    mm.then_inc(pe_done, 1)
                pe.wait_ge(evac, plan["w1"]["t0"] + 2 * kv + 2)
                if kv == 0:
                    c0 = ncol["w2k"][0]
                    for hh in range(2):
                        mm = pe.matmul(ps[:, 4, 0:124], npar[:, c0 + P * hh:c0 + P * hh + P], hid[:, hh],
                                       start=hh == 0, stop=hh == 1)
                else:
                    c0 = ncol["w2v"][0]
                    for g in range(NSA_GROUPS):
                        for hh in range(2):
                            mm = pe.matmul(ps[0:CMP_N, 5, HD * g:HD * g + HD], hid[:, hh, CMP_N * g:CMP_N * g + CMP_N],
                                           npar[:, c0 + HD * hh:c0 + HD * hh + HD], start=hh == 0, stop=hh == 1)
                mm.then_inc(c_mm, 1)

            def nsa_scores(gp, t, u):
                pr, b, br = u // 6, u // 3 % 2, u % 3
                g = 2 * gp + b
                rows = slice(HD * b, HD * b + HD)
                pe.wait_ge(a_q, 2 * t + (4 * gp + pr + 1))
                pe.wait_ge(a_mx, 48 * t + (96 * gp + 4 * u))
                for n, qts in enumerate(((3,), (0, 2), (1,)) if br < 2 else ((0, 1, 2, 3),)):
                    for qt in qts:
                        at_, w = dict(nsa_rows(u))[qt]
                        keys = f1[rows, 12 + 2 * br + gp, 0:w] if br < 2 else kcmp[rows, CMP_N * g:CMP_N * g + w]
                        mm = pe.matmul(ps[:, n, at_ - BANKS[n][0]:at_ - BANKS[n][0] + w],
                                       q_st[rows, pr, P * qt:P * qt + P], keys, start=True, stop=True,
                                       skip_group_check=True)
                    mm.then_inc(a_s, 1)

            def nsa_turn(gp, t, u):
                pe.wait_ge(a_n, 48 * t + (96 * gp + 4 * u + 4))
                pe.wait_ge(a_pt, 28 * t + (56 * gp + T_BEFORE[u]))
                r = u % 3
                if u % 3 < 2:
                    for n, tiles in enumerate(((0,), (1, 3), (2,))):
                        for kt in tiles:
                            for qt in range(kt, NT):
                                off = KOFF[kt] - BANKS[n][0] + P * (qt - kt)
                                mm = pe.transpose(ps[:, 3 + n, off:off + P],
                                                  s_p[:, r, QOFF[qt] + P * kt:QOFF[qt] + P * kt + P], ident)
                        mm.then_inc(a_t, 1)
                else:
                    for qt, (at_, w) in nsa_rows(u):
                        mm = pe.transpose(ps[0:w, 3, P * qt:P * qt + P], s_p[:, r, at_:at_ + w], ident)
                    mm.then_inc(a_t, 1)

            def nsa_values(gp, t, u):
                pr, b, br = u // 6, u // 3 % 2, u % 3
                g = 2 * gp + b
                pe.wait_ge(a_pt, 28 * t + (56 * gp + T_BEFORE[u + 1]))
                if u % 6 == 0:
                    pe.wait_ge(a_mix, 4 * t + 8 * gp)
                out = ps[HD * b:HD * b + HD, 6 + pr, :]
                if br < 2:
                    for kt in range(NT):
                        c0 = 256 * br + HD * g
                        mm = pe.matmul(out[:, P * kt:], v1[:, kt, c0:c0 + HD],
                                       p_t[:, u % 2, KOFF[kt]:KOFF[kt] + SEQ - P * kt],
                                       start=br == 0 and kt == 0, stop=False, skip_group_check=True)
                else:
                    for qt, (at_, w) in nsa_rows(u):
                        mm = pe.matmul(out[:, P * qt:P * qt + P], vcmp[0:w, HD * g:HD * g + HD],
                                       p_t[0:w, u % 2, P * qt:P * qt + P], start=False, stop=qt == NT - 1,
                                       skip_group_check=True)
                mm.then_inc(a_pv, 1)

            pe.wait_ge(c_out, 2)
            pe.wait_ge(gt_ac, 1)
            for gp in range(2):
                with pe.Fori(0, 2) as t:
                    for v in range(15):
                        if v < 12:
                            nsa_scores(gp, t, v)
                        if 2 <= v < 14:
                            nsa_turn(gp, t, v - 2)
                        if v >= 3:
                            nsa_values(gp, t, v - 3)

            pe.wait_ge(a_mix, 16)
            with pe.Fori(0, 2) as t:
                for s in range(2):
                    features("out1", 2 * t + s, s, mix1)
            out_sums(2)
            ffn(1)

        @block.vector
        def _(ve):
            def ada_chunk(a, s, nth, buf, acc):
                ve.wait_ge(ada_landed[s], 16 * nth)
                wait(ve, ada_mm, a - 1)
                for k in range(KT):
                    if k == 0:
                        ve.tensor_scalar(acc[:, s], buf[:, s, k], cond[:, 0:1], None, ALU.mult).then_inc(ada_sum, 1)
                    else:
                        ve.wait_ge(ada_sum, 8 * a + k)
                        ve.scalar_tensor_tensor(acc[:, s], buf[:, s, k], cond[:, k:k + 1], acc[:, s],
                                                ALU.mult, ALU.add).then_inc(ada_sum, 1)

            def modulation(lo, hi):
                ve.wait_ge(ada_mm, hi // 2)
                ve.tensor_tensor(modc[:, lo:hi], ps[:, 7, lo:hi], par[:, pcol["ada_b"][0] + lo:pcol["ada_b"][0] + hi],
                                 ALU.add).then_inc(mod_ready, 1)

            def a_gain(i):
                c = 48 * (i // 2) + 24 * (i % 2) + 8
                g = pcol["norm_g"][0] + 16 * i
                ve.scalar_tensor_tensor(gains[:, 16 * i:16 * i + 8], modc[:, c:c + 8], 1.0, par[:, g:g + 8],
                                        ALU.add, ALU.mult).then_inc(mod_ready, 1)

            def g_gain(i):
                c = 48 * (i // 2) + 24 * (i % 2) + 16
                g = pcol["norm_g"][0] + 16 * i + 8
                ve.tensor_tensor(gains[:, 16 * i + 8:16 * i + 16], modc[:, c:c + 8], par[:, g:g + 8],
                                 ALU.mult).then_inc(mod_ready, 1)

            def norm_in(i):
                s = norms[i]
                ve.wait_ge(n_rs, RS_IN[i] + 2)
                for k in range(KT):
                    if k >= 2:
                        ve.wait_ge(n_lo, 8 * i + k - 1)
                    ve.tensor_tensor(s["hm"][:, k % 2], x[:, k], s["rstd"][:, :], ALU.mult).then_inc(n_dv, 1)
                    ve.wait_ge(n_dv, 16 * i + 2 * k + 1)
                    ve.tensor_scalar(s["hm"][:, k % 2], s["hm"][:, k % 2], a_col(i, k), shift_col(i, k),
                                     ALU.mult, ALU.add).then_inc(n_dv, 1)

            def y_start(p):
                ve.memset(posts[p]["ssum"][:, :], 0.0).then_inc(y_sum, 1)

            def y_square(p, tile0, x_, par_):
                s = posts[p]
                ve.wait_ge(evac, x_ + (tile0 + 1))
                ve.wait_ge(y_sum, x_ + (9 * p + 1))
                ve.tensor_tensor(s["ssum"][:, :], s["ssum"][:, :], s["sq"][:, par_], ALU.add).then_inc(y_sum, 1)

            def residual(p):
                s, y = posts[p], ys[p]
                ve.wait_ge(n_rs, RS_OUT[p] + 2)
                for k in range(KT):
                    ve.scalar_tensor_tensor(y[:, k], y[:, k], g_col(p, k), s["rstd"][:, :],
                                            ALU.mult, ALU.mult).then_inc(res, 1)
                    ve.wait_ge(res, 16 * p + 2 * k + 1)
                    ve.tensor_tensor(x[:, k], x[:, k], y[:, k], ALU.add).then_inc(res, 1)

            def taps(out, src, w_col, b_col, width, done, at_):
                first = PAD - width + 1
                ve.tensor_scalar(out, src[:, first + width - 1:first + width - 1 + SEQ], w_col(width - 1), b_col,
                                 ALU.mult, ALU.add).then_inc(done, 1)
                for j in range(width - 2, -1, -1):
                    ve.wait_ge(done, at_ + (width - 1 - j))
                    ve.scalar_tensor_tensor(out, src[:, first + j:first + j + SEQ], w_col(j), out,
                                            ALU.mult, ALU.add).then_inc(done, 1)

            def ffn(l):
                name = f"up{l}"
                for n in range(4):
                    ve.memset(ub[:, n, 0:PAD], 0.0).then_inc(pad, 1)
                ve.wait_ge(pad, 4 * (2 + l))
                with ve.Fori(0, FT // 2) as t:
                    for s in range(2):
                        base = 18 * t + (9 * FT * l + 9 * s)
                        for half, out in ((0, cg[:, s]), (1, cv[:, :])):
                            ve.wait_ge(evac, 4 * t + (plan[name]["t0"] + 2 * s + half + 1))
                            i = 2 * t + (s + FT * half)
                            taps(out, ub[:, 2 * s + half], lambda j: pc(f"fconv_w{l}", 3 * i + j),
                                 pc(f"fconv_b{l}", i), 3, f_dv, base + 3 * half)
                        ve.wait_ge(f_gelu, 2 * t + (FT * l + s + 1))
                        ve.wait_ge(f_dv, base + 6)
                        ve.tensor_tensor(cv[:, :], cg[:, s], cv[:, :], ALU.mult).then_inc(f_dv, 1)
                        ve.wait_ge(f_dv, base + 7)
                        j = 2 * t + s
                        ve.tensor_copy(act[:, 0, bass.ds(j, 1), :], cv[:, :].unsqueeze(1)).then_inc(f_dv, 1)
                        ve.wait_ge(f_dv, base + 8)
                        ve.tensor_tensor(act[:, 1, bass.ds(j, 1), :], cv[:, :].unsqueeze(1),
                                         act[:, 0, bass.ds(j, 1), :].bitcast(F32), ALU.subtract).then_inc(f_dv, 1)
                ve.wait_ge(f_dv, 9 * FT * (l + 1))
                y_start(1 + 2 * l)
                tile0 = plan[f"down{l}"]["t0"]
                with ve.Fori(0, 4) as t:
                    for c in range(4):
                        if l == 0:
                            ada_chunk(6 * t + (24 + c), c % 2, 3 * t + (13 + c // 2), ada_in1, ada_acc1)
                        if c % 2:
                            y_square(1 + 2 * l, tile0, 2 * t + c // 2, c // 2)
                    if l == 0:
                        for c in range(2):
                            ada_chunk(6 * t + (28 + c), c, 3 * t + 15, ada_in1, ada_acc1)

            ve.memset(relt[32:33, :], NEG).then_inc(setup, 1)
            ve.memset(one[:, :], 1.0).then_inc(setup, 1)
            for n in range(4):
                ve.memset(ub0[:, n, 0:PAD], 0.0).then_inc(pad, 1)
            ve.wait_ge(const_in, 96)
            ve.tensor_copy(cr[:, :, :].rearrange("p a b -> p (a b)"),
                           dm[:, :, :].rearrange("p a b -> p (a b)")[:, 0:5 * P]).then_inc(setup, 1)
            ve.tensor_copy(wdt[:, 0], wdt_f[:, :, :]).then_inc(setup, 1)
            ve.wait_ge(setup, 4)
            ve.tensor_tensor(wdt[:, 1], wdt_f[:, :, :], wdt[:, 0].bitcast(F32), ALU.subtract).then_inc(setup, 1)
            for n in range(2):
                ve.wait_ge(table_mm, n + 1)
                ve.tensor_copy(table[:, 320 * n:320 * n + 320], ps[0:16, n, 0:320]).then_inc(table_out, 1)
            ve.wait_ge(cond_ready, 1)
            for a in range(ADA_FIRST):
                ada_chunk(a, a % 2, a // 2 + 1, ada_in0, ada_acc0)
            modulation(0, 16)
            ve.wait_ge(mod_ready, 1)
            a_gain(0)
            ve.wait_ge(mod_ready, 2)
            ve.wait_ge(x_in, 16)
            norm_in(0)

            def ada_pair(t, at_):
                for s in range(2):
                    ada_chunk(2 * t + (at_ + s), s, t + (at_ // 2 + 1), ada_in0, ada_acc0)

            for at_ in (8, 10):
                with ve.Fori(0, 1) as t:
                    ada_pair(t, at_)

            def xbc(t):
                for n in range(4):
                    x_ = 4 * t + n
                    ve.wait_ge(evac, x_ + (plan["xbc"]["t0"] + 1))
                    wait(ve, silu_x, x_ - 1)
                    taps(cacc0[:, n % 2], ub0[:, n], lambda j: pc("conv_w", 4 * x_ + j), pc("conv_b", x_), 4,
                         conv, 4 * x_)
                    if n % 2:
                        a = 2 * t + (12 + n // 2)
                        ada_chunk(a, n // 2, t + 7, ada_in0, ada_acc0)

            ve.wait_ge(pad, 4)
            xbc(0)
            with ve.Fori(1, 4) as t:
                xbc(t)
            with ve.Fori(0, 2) as t:
                ada_pair(t, 20)
            modulation(16, 48)
            ve.wait_ge(mod_ready, 3)
            g_gain(0)
            a_gain(1)
            g_gain(1)

            def heads(name):
                return par[:, pcol[name][0]:pcol[name][0] + 16]

            def over_tiles(ap):
                return ap.unsqueeze(1).to_broadcast([P, NT, 16])

            ve.wait_ge(dt_mm, 1)
            ve.tensor_tensor(dt_raw, ps[:, 6, 0:64].rearrange("p (t h) -> p t h", t=NT), over_tiles(heads("dt_bias")),
                             ALU.add).then_inc(dt_dv, 1)
            ve.wait_ge(dt_dv, 1)
            ve.scalar_tensor_tensor(dt_l, dt_raw, -1.0, dt_raw, ALU.mult, ALU.min).then_inc(dt_dv, 1)
            ve.wait_ge(dt_ac, 3)
            ve.scalar_tensor_tensor(dt_v, dt_raw, 0.0, dt_l, ALU.max, ALU.add).then_inc(dt_dv, 1)
            ve.tensor_scalar(dts[:, 6, 1, :], dts[:, 6, 0, :], -1.0, None, ALU.mult).then_inc(dt_dv, 1)
            ve.wait_ge(dt_dv, 4)
            ve.tensor_tensor(dt_a, dt_v, over_tiles(dts[:, 6, 1, :]), ALU.mult).then_inc(dt_dv, 1)

            def sb_softplus(u):
                ve.wait_ge(sb_e, 2 * u + 2)
                for n, (at_, w) in enumerate(BANKS):
                    l = sb_l[:, u % 2, at_:at_ + w]
                    ve.scalar_tensor_tensor(l, ps[:, 3 * (u % 2) + n, 0:w], 0.0, l, ALU.max, ALU.add).then_inc(sb_L, 1)
                ve.wait_ge(sb_L, 3 * u + 3)
                if u >= 2:
                    ve.wait_ge(sb_s, 3 * (u - 1))
                ve.tensor_copy(sb_lr[:, u % 2, 0], sb_l[:, u % 2]).then_inc(sb_hi, 1)

            def sb_out(i):
                ve.wait_ge(sb_pv, 2 * i + 2)
                ve.tensor_copy(mix_sb[:, 0, i], ps[:, 6 + i % 2, :]).then_inc(sb_mix, 1)
                ve.wait_ge(sb_mix, 2 * i + 1)
                ve.tensor_tensor(mix_sb[:, 1, i], ps[:, 6 + i % 2, :], mix_sb[:, 0, i].bitcast(F32),
                                 ALU.subtract).then_inc(sb_mix, 1)

            ve.wait_ge(dt_mm, 3)
            ve.tensor_copy(dt_acs, ps[:, 7, 0:64].rearrange("p (t h) -> p t h", t=NT)).then_inc(dt_dv, 1)
            ve.wait_ge(dt_ac, 4)
            ve.tensor_tensor(dt_w, dt_w, dt_v, ALU.mult).then_inc(dt_dv, 1)
            ve.wait_ge(dt_tr, 1)
            ve.tensor_copy(acs[:, :], ps[0:16, 6, :]).then_inc(dt_dv, 1)
            sb_softplus(0)
            sb_softplus(1)
            for u in range(SB_HEADS):
                if u + 2 < SB_HEADS:
                    sb_softplus(u + 2)
                if u >= 2 and u % 2 == 0:
                    sb_out(u // 2 - 1)
            sb_out(3)

            def per_head(i, c0, n, g):
                return dts[:, i, c0:c0 + n, 4 * g:4 * g + 4].unsqueeze(3).to_broadcast([P, n, 4, HD])

            def cols(ap):
                return ap.rearrange("p c (h d) -> p c h d", d=HD)

            ve.wait_ge(dt_dv, 8)
            for g in range(SSM_GROUPS):
                if g:
                    ve.wait_ge(hd_y, 4 * g)
                for n in range(2):
                    ve.wait_ge(g_pe, 5 * g + 2 + n)
                    src = ps[:, 1 + n, :].rearrange("p (c f) -> p c f", c=2)
                    ve.tensor_tensor(cols(xdt[:, 2 * n:2 * n + 2]), cols(src), per_head(2, 2 * n, 2, g),
                                     ALU.mult).then_inc(g_dv, 1)
                    m = 2 - n
                    ve.tensor_tensor(cols(xw[:, 2 * n:2 * n + m]), cols(src[:, 0:m]), per_head(5, 2 * n, m, g),
                                     ALU.mult).then_inc(g_dv, 1)
                for hh in range(4):
                    n = 4 * g + hh
                    ve.wait_ge(hd_mask, n + 1)
                    if n >= 2:
                        ve.wait_ge(hd_y, n - 1)
                    ve.tensor_tensor(dm[:, n % 2].rearrange("p (c l) -> p c l", c=NT),
                                     ps[:, 6 + n % 2, :].rearrange("p (c l) -> p c l", c=NT),
                                     dt_acs[:, :, n:n + 1].to_broadcast([P, NT, P]), ALU.subtract).then_inc(hd_d, 1)
                    ve.wait_ge(hd_x, n + 1)
                    ve.wait_ge(g_ac, 3 * g + 3)
                    ve.tensor_tensor(dm[:, n % 2], dm[:, n % 2], cb[:, :], ALU.mult).then_inc(hd_dv, 1)
                    ve.tensor_tensor(cs[:, n % 2], xs[:, 12 + g, P:], eb[:, n % 2, P:], ALU.mult).then_inc(hd_dv, 1)
                    for c, (bank, off) in ((1, (4, 256)), (2, (5, 0))):
                        if c == 2:
                            ve.wait_ge(hd_dv, 4 * n + 3)
                        hs = slice(HD * hh, HD * hh + HD)
                        ve.scalar_tensor_tensor(st[:, c, hs], st[:, c - 1, hs],
                                                eb[:, n % 2, P * (c + 1) - 1:P * (c + 1)],
                                                ps[:, bank, off + HD * hh:off + HD * hh + HD],
                                                ALU.mult, ALU.add).then_inc(hd_dv, 1)
                    if hh % 2:
                        k = 2 * g + hh // 2
                        ve.wait_ge(hd_y, 2 * k + 2)
                        col = pcol["d_skip"][0] + k
                        ve.scalar_tensor_tensor(yt[:, :], xs[:, k], par[:, col:col + 1], ps[:, 1 + hh // 2, :],
                                                ALU.mult, ALU.add).then_inc(yg, 1)
                        ve.wait_ge(yg, 3 * k + 1)
                        ve.tensor_tensor(zs[:, k], yt[:, :], zs[:, k], ALU.mult).then_inc(yg, 1)
                        ve.wait_ge(ms_sq, k + 1)
                        if k == 0:
                            ve.tensor_copy(s_low["ssum"][:, :], s_low["sq"][:, 0]).then_inc(yg, 1)
                        else:
                            ve.tensor_tensor(s_low["ssum"][:, :], s_low["ssum"][:, :], s_low["sq"][:, k % 2],
                                             ALU.add).then_inc(yg, 1)
            ve.wait_ge(n_rs, RS_SSM + 2)
            for k in range(8):
                col = pcol["ssm_norm"][0] + k
                if k >= 2:
                    ve.wait_ge(ms_lo, k - 1)
                ve.scalar_tensor_tensor(s_low["hm"][:, k % 2], zs[:, k], par[:, col:col + 1], s_low["rstd"][:, :],
                                        ALU.mult, ALU.mult).then_inc(ms_dv, 1)
                ve.wait_ge(ms_dv, 2 * k + 1)
                ve.tensor_copy(mix_ssm[:, 0, k], s_low["hm"][:, k % 2]).then_inc(ms_dv, 1)

            y_start(0)
            with ve.Fori(0, 4) as t:
                for s in range(2):
                    y_square(0, plan["out0"]["t0"], 2 * t + s, s)
            residual(0)
            norm_in(1)
            ffn(0)
            modulation(48, 96)
            ve.wait_ge(mod_ready, 7)
            for i in (2, 3):
                a_gain(i)
                g_gain(i)
            ve.wait_ge(mod_ready, 11)
            residual(1)

            norm_in(2)
            ve.wait_ge(npar_in, 16)
            src = npar[:, ncol["w_gate"][0]:ncol["w_gate"][0] + 384].rearrange("p (k c) -> p k c", k=KT)
            ve.tensor_copy(wg_r[:, 0], src).then_inc(gt_w, 1)
            ve.wait_ge(gt_w, 1)
            ve.tensor_tensor(wg_r[:, 1], src, wg_r[:, 0].bitcast(F32), ALU.subtract).then_inc(gt_w, 1)
            for kv in range(2):
                ve.wait_ge(shift_in, 128 * (kv + 1))
                wait(ve, fl_lo, kv)
                for i in range(16):
                    col = ncol["pe"][0] + 16 * kv + i
                    ve.tensor_scalar(fl[:, i, :].rearrange("p (g n) -> p g n", g=NSA_GROUPS),
                                     kcs[:, :, 2 * i:2 * i + 16 * (CMP_N - 1) + 1:16], npar[:, col:col + 1], None,
                                     ALU.add).then_inc(fl_dv, 1)
            ve.wait_ge(c_mm, 1)
            ve.tensor_copy(kcmp[:, :], ps[:, 4, 0:124]).then_inc(c_out, 1)
            ve.wait_ge(c_mm, 2)
            ve.tensor_copy(vcmp[:, :], ps[0:CMP_N, 5, 0:256]).then_inc(c_out, 1)
            ve.wait_ge(gt_ac, 1)
            ve.tensor_scalar(gates[:, :, :], gates[:, :, :], 1.0, None, ALU.add).then_inc(gt_dv, 1)
            ve.wait_ge(gt_dv, 1)
            ve.reciprocal(gates[:, :, :], gates[:, :, :]).then_inc(gt_dv, 1)
            ve.wait_ge(gt_dv, 2)

            def nsa_max(gp, t, u):
                pr, b, r = u // 6, u // 3 % 2, u % 3
                for i, (qt, (at_, w)) in enumerate(nsa_rows(u)):
                    n = (1, 2, 1, 0)[qt] if u % 3 < 2 else 0
                    ve.reg_add(scores, scores_before, 56 * gp + T_BEFORE[u] + n + 1)
                    if i == 0:
                        ve.reg_add(turned, scores_before, 56 * gp + T_BEFORE[max(0, u - 2)])
                    ve.wait_ge(gt_dv, 2)
                    if i == 0:
                        ve.wait_ge(a_t, turned)
                    ve.wait_ge(a_s, scores)
                    bias = u_b[:, pr, b, 384 - P * qt:] if u % 3 < 2 else u_b[:, pr, b, 415 - P * qt::16]
                    ve.tensor_tensor_reduce(s_p[:, r, at_:at_ + w], ps[:, n, at_ - BANKS[n][0]:at_ - BANKS[n][0] + w],
                                            bias, 1.0, -3e38, ALU.add, ALU.max, mx[:, r, qt:qt + 1]).then_inc(a_mx, 1)
                ve.wait_ge(a_mx, 48 * t + (96 * gp + 4 * u + 4))
                ve.tensor_scalar(mx[:, r], mx[:, r], -1.0, 1e29, ALU.mult, ALU.min).then_inc(a_neg, 1)

            def nsa_scale(gp, t, u):
                pr, b, br, r = u // 6, u // 3 % 2, u % 3, u % 3
                ve.wait_ge(a_p, 48 * t + (96 * gp + 4 * u + 4))
                base = 36 * t + (72 * gp + 3 * u)
                ve.tensor_scalar(sc[:, r], rs[:, r], 1e-30, None, ALU.max).then_inc(a_sc, 1)
                ve.wait_ge(a_sc, base + 1)
                ve.reciprocal(sc[:, r], sc[:, r]).then_inc(a_sc, 1)
                ve.wait_ge(a_sc, base + 2)
                gate = gates[:, bass.ds(6 * t + (3 * (8 * gp + 4 * b + pr) + (1, 2, 0)[br]), 1), :]
                ve.tensor_tensor(sc[:, r:r + 1], sc[:, r:r + 1], gate, ALU.mult).then_inc(a_sc, 1)
                ve.wait_ge(a_sc, base + 3)
                for qt, (at_, w) in nsa_rows(u):
                    ve.tensor_scalar(s_p[:, r, at_:at_ + w], s_p[:, r, at_:at_ + w], sc[:, r, qt:qt + 1], None,
                                     ALU.mult).then_inc(a_n, 1)

            def nsa_out(gp, t, pr):
                ve.wait_ge(a_pv, 12 * t + (24 * gp + 6 * pr + 6))
                j = 2 * t + (4 * gp + pr)
                ve.tensor_copy(mix1[:, 0, bass.ds(j, 1), :], ps[:, 6 + pr:7 + pr, :]).then_inc(a_mix, 1)
                ve.wait_ge(a_mix, 4 * t + (8 * gp + 2 * pr + 1))
                ve.tensor_tensor(mix1[:, 1, bass.ds(j, 1), :], ps[:, 6 + pr:7 + pr, :],
                                 mix1[:, 0, bass.ds(j, 1), :].bitcast(F32), ALU.subtract).then_inc(a_mix, 1)

            scores_before, scores, turned = (ve.alloc_register(k) for k in ("scores_before", "scores", "turned"))
            for gp in range(2):
                with ve.Fori(0, 2) as t:
                    ve.reg_mul(scores_before, t, 28)
                    ve.wait_ge(a_s, 28 * t + 56 * gp)
                    ve.wait_ge(u_in[0], 16 * t + (32 * gp + 16))
                    for pr in range(2):
                        ve.tensor_copy(q_st[:, pr:pr + 1], f1[:, bass.ds(2 * t + (4 * gp + pr), 1), :]).then_inc(a_q, 1)
                    for v in range(15):
                        if v < 12:
                            nsa_max(gp, t, v)
                        if v == 5:
                            ve.wait_ge(u_in[1], 16 * t + (32 * gp + 16))
                        if 1 <= v < 13:
                            nsa_scale(gp, t, v - 1)
                        if v == 10:
                            nsa_out(gp, t, 0)
                        if v == 14:
                            nsa_out(gp, t, 1)

            y_start(2)
            with ve.Fori(0, 2) as t:
                for n in range(4):
                    y_square(2, plan["out1"]["t0"], 4 * t + n, n % 2)
            residual(2)
            norm_in(3)
            ffn(1)
            residual(3)


_OUT = (DM, SEQ)


def _layout(i):
    import math

    import numpy as np

    f = np.float32
    eye = np.eye(P, dtype=f)
    p, q = np.arange(P)[:, None], np.arange(P)[None, :]
    consts = np.stack([
        eye, np.full((P, P), 1.0 / DM, f), (p <= q).astype(f), (p > q).astype(f),
        eye, -(p >= q).astype(f), np.full((P, P), -1.0, f),
        np.where(p >= q, f(NEG), f(0)).astype(f), np.where(p > q, f(NEG), f(0)).astype(f)], axis=1)

    dist = np.arange(SEQ)
    nf = np.maximum(dist, 1).astype(f)
    large = np.minimum(16 + (np.log(nf / f(16)) / f(math.log(64)) * f(16)).astype(np.int32), REL_BUCKETS - 1)
    bucket = np.where(dist < 16, dist, large)
    onehot = np.zeros((33, 640), f)
    onehot[bucket[511 - np.arange(SEQ)], np.arange(SEQ)] = 1
    onehot[32, SEQ:] = 1

    def cols(a):
        return a.reshape(-1, P).T

    def put(columns, total, values):
        out = np.zeros((P, total), f)
        for name, v in values.items():
            at, n = columns[name]
            out[:, at:at + n] = v
        return out

    conv_w, fw, fb = i["ab_conv_w"][0], i["ffn_conv_w"], i["ffn_conv_b"]
    pcols, n_p = param_columns()
    params = put(pcols, n_p, {
        "ada_b": cols(i["ada_b"]), "norm_g": cols(i["norm_g"]),
        "conv_w": conv_w.reshape(4, 16, P).transpose(2, 1, 0).reshape(P, 64), "conv_b": cols(i["ab_conv_b"][0]),
        "d_skip": cols(np.repeat(i["ab_d_skip"][0], HD)), "ssm_norm": cols(i["ab_ssm_norm"][0]),
        "fconv_w0": fw[0].reshape(3, 44, P).transpose(2, 1, 0).reshape(P, 132),
        "fconv_w1": fw[1].reshape(3, 44, P).transpose(2, 1, 0).reshape(P, 132),
        "fconv_b0": cols(fb[0]), "fconv_b1": cols(fb[1]),
        "dt_bias": np.broadcast_to(i["ab_dt_bias"][0], (P, 16)), "a_log": np.broadcast_to(i["ab_a_log"][0], (P, 16)),
        "cond": cols(i["c"][0])})

    def out_tiles(w, kt, per):
        n = w.shape[1] // P
        return w.reshape(kt, P, n, P).transpose(2, 1, 0, 3).reshape(n // per, per, P, kt * P).transpose(0, 2, 1, 3) \
            .reshape(n // per, P, per * kt * P)

    def rows512(w):
        return w.reshape(2, 4, P, SEQ).transpose(0, 2, 1, 3).reshape(2, P, CW)

    w_in, w_nsa = i["ab_w_in"][0], i["nsa_w_in"][0]
    f0 = np.concatenate([w_in[:, 0:1024], w_in[:, 2560:4608], w_in[:, 1536:2560]], axis=1)
    w_dt = w_in[:, 4608:4624].reshape(KT, P, 16).transpose(1, 0, 2)
    heads = [8 * (j // 4) + j % 4 + 4 * b for j in range(8) for b in range(2)]
    wq = w_nsa[:, 0:1024].reshape(DM, 16, HD)[:, heads].reshape(DM, 1024)
    f1 = np.concatenate([wq, w_nsa[:, 1024:1536], w_nsa[:, 1536:1792], w_nsa[:, 2048:2304]], axis=1)
    v1 = np.concatenate([w_nsa[:, 1792:2048], w_nsa[:, 2304:2560]], axis=1)
    w_o1 = i["nsa_w_out"][0].reshape(16, HD, DM)[heads].reshape(1024, DM)
    w1, w2, pe = i["nsa_cmp_w1"][0], i["nsa_cmp_w2"][0], i["nsa_cmp_pe"][0]
    w2k = w2[0].reshape(2, P, HD).transpose(1, 0, 2)
    ncols, n_n = nsa_columns()
    nsa_params = put(ncols, n_n, {
        "w2k": np.concatenate([w2k, w2k], axis=2).reshape(P, 256),
        "w2v": w2[1].reshape(2, P, HD).transpose(1, 0, 2).reshape(P, 128),
        "w_gate": w_nsa[:, 2560:2608].reshape(KT, P, 48).transpose(1, 0, 2).reshape(P, 384),
        "pe": pe.reshape(2, 16, P).transpose(2, 0, 1).reshape(P, 32),
        "b1": cols(i["nsa_cmp_b1"][0])})
    up = i["ffn_w_up"].reshape(2, KT, P, 2, FT, P).transpose(0, 4, 2, 3, 1, 5).reshape(2 * FT, P, CW)
    down = i["ffn_w_down"].reshape(2, 2, 11, P, KT, P).transpose(0, 4, 1, 3, 2, 5).reshape(32, P, 11 * P)
    ada = i["ada_w"].reshape(2, KT, P, ADA_N, ADA_W).transpose(0, 3, 2, 1, 4).reshape(2 * ADA_N, P, KT, ADA_W)
    return [
        i["x"][0].T, consts, params, nsa_params, w_dt, onehot, i["rel_bias"].T, ada,
        rows512(w_in[:, 1024:1536]), out_tiles(f0, KT, 2), out_tiles(i["ab_w_out"][0], 12, 1),
        rows512(v1), out_tiles(f1, KT, 2),
        w1.reshape(2, 2, 8, P, 256).transpose(0, 1, 3, 2, 4).reshape(4, P, CW),
        out_tiles(w_o1, KT, 2), up, down]


def kernel(**inputs):
    import numpy as _np
    import concourse.bacc as _bacc
    from concourse import mybir as _mybir
    from concourse.bass_utils import run_bass_kernel_spmd as _run

    nc = _bacc.Bacc("TRN2", target_bir_lowering=False, num_devices=1)
    arrays, args = {}, []
    for n, a in enumerate(_layout({k: _np.asarray(v) for k, v in inputs.items()})):
        a = _np.ascontiguousarray(a)
        arrays[f"in_{n}_dram"] = a
        args.append(nc.dram_tensor(f"in_{n}_dram", a.shape, _mybir.dt.from_np(a.dtype), kind="ExternalInput").ap())
    out = nc.dram_tensor("out_0_dram", _OUT, _mybir.dt.float32, kind="ExternalOutput").ap()
    trunk(nc, *args, out)
    r = _run(nc, [arrays], core_ids=[0])
    return _np.ascontiguousarray(r.results[0]["out_0_dram"].T)[None]
```

```python
from contextlib import ExitStack

import concourse.bass as bass
from concourse import mybir

P = 128
F32 = mybir.dt.float32
F32R = mybir.dt.float32r
ALU = mybir.AluOpType
ACT = mybir.ActivationFunctionType

SEQ, DM = 512, 1024
NT = SEQ // P
KT = DM // P
SB_HEADS, HD = 8, 64
SSM_HEADS, SSM_GROUPS = 16, 4
NSA_GROUPS = 4
CMP_N = SEQ // 16 - 1
D_FF = 2816
FT = D_FF // P
REL_BUCKETS = 32
EPS = 1e-6
NEG = -1e30
CH = 16
CW = CH * P
ADA_W = 256
ADA_N = 6 * DM // ADA_W
ADA_FIRST = 2 * DM // ADA_W
HM = 4
UB = SEQ + 4
PAD = 4
KOFF = (0, 512, 1024, 896)
QOFF = (512, 1024, 640, 0)
BANKS = ((0, 512), (512, 512), (1024, 256))


def param_columns():
    sizes = [("ada_b", 96), ("norm_g", 64), ("conv_w", 64), ("conv_b", 16), ("d_skip", 8), ("ssm_norm", 8),
             ("fconv_w0", 132), ("fconv_w1", 132), ("fconv_b0", 44), ("fconv_b1", 44),
             ("dt_bias", 16), ("a_log", 16), ("cond", 8)]
    at, cols = 0, {}
    for name, n in sizes:
        cols[name] = (at, n)
        at += n
    return cols, at


def nsa_columns():
    sizes = [("w2k", 256), ("w2v", 128), ("w_gate", 384), ("pe", 32), ("b1", 4)]
    at, cols = 0, {}
    for name, n in sizes:
        cols[name] = (at, n)
        at += n
    return cols, at


def chunk_plan():
    rows = [("v0", 2, 16, 0), ("q", 2, 16, 2), ("k", 2, 16, 2), ("xbc", 8, 16, 2), ("z", 4, 16, 2),
            ("out0", 8, 12, 1), ("up0", 22, 16, 2), ("down0", 16, 11, 1),
            ("v1", 2, 16, 0), ("f1", 8, 16, 2), ("w1", 4, 16, 1), ("out1", 4, 16, 2),
            ("up1", 22, 16, 2), ("down1", 16, 11, 1)]
    tiles = {"v0": 4, "v1": 4, "w1": 4, "down0": 8, "down1": 8}
    plan, c, ev, tile, extra = {}, 0, 0, 0, 0
    for name, n, size, per in rows:
        plan[name] = dict(c0=c, n=n, size=size, per=per, ev0=ev, t0=tile, extra=extra)
        c += n
        ev += n * per if per else 5
        tile += tiles.get(name, n * per)
        if size < CH and name != "down1":
            extra += 1
    return plan


def trunk(nc, x_t, consts, params, nsa_params, w_dt, onehot, relb, ada, w_v0, w_f0, w_out0, w_v1, w_f1, w_c1,
          w_out1, w_up, w_down, out_t):
    plan = chunk_plan()
    pcol, NP = param_columns()
    ncol, NN = nsa_columns()
    weights = {"v0": (w_v0, 0), "q": (w_f0, 0), "k": (w_f0, 2), "xbc": (w_f0, 4), "z": (w_f0, 12),
               "out0": (w_out0, 0), "up0": (w_up, 0), "down0": (w_down, 0), "v1": (w_v1, 0), "f1": (w_f1, 0),
               "w1": (w_c1, 0), "out1": (w_out1, 0), "up1": (w_up, 22), "down1": (w_down, 16)}

    ctx = ExitStack()
    with ctx:
        start = -(-nc.sbuf_base // 64) * 64
        top = [0]

        def at(name, shape, dt, offset):
            n = 4
            for d in shape[1:]:
                n *= d
            top[0] = max(top[0], offset + n)
            return nc.alloc_sbuf_tensor_at(name, shape, dt, offset=offset)

        o = start
        fixed = {}
        for name, shape, dt in [
            ("x", [P, KT, SEQ], F32), ("raw", [P, 2, CW], F32), ("ring", [P, 2, 2, CW], F32R),
            ("cf", [P, 4, P], F32), ("cr", [P, 5, P], F32R), ("par", [P, NP], F32), ("modc", [P, 96], F32),
            ("gains", [P, 64], F32), ("cond", [P, KT], F32), ("one", [P, 1], F32),
        ]:
            fixed[name] = at(name, shape, dt, o)
            n = 4
            for d in shape[1:]:
                n *= d
            o += -(-n // 32) * 32
        x, raw, ring, cf, cr, par = (fixed[k] for k in ("x", "raw", "ring", "cf", "cr", "par"))
        modc, gains, cond, one = (fixed[k] for k in ("modc", "gains", "cond", "one"))
        ident, mean_of, tri_le, tri_gt = (cf[:, i, :] for i in range(4))
        ident_r, neg_suffix, neg_ones, mask_sb, mask_ssd = (cr[:, i, :] for i in range(5))
        H = o
        R = H + 32768
        K = 1024
        h = at("h", [P, 2, KT, SEQ], F32R, H)

        def scratch(tag, base):
            return dict(rstd=at("rstd" + tag, [P, SEQ], F32, base), ssum=at("ssum" + tag, [P, SEQ], F32, base + 2 * K),
                        sq=at("sq" + tag, [P, 2, SEQ], F32, base + 4 * K),
                        hm=at("hm" + tag, [P, HM, SEQ], F32, base + 8 * K))

        s_low, s_high = scratch("_low", R), scratch("_high", R + 88 * K)

        qk0 = at("qk0", [P, 8, SEQ], F32, R)
        v0 = at("v0", [P, NT, SEQ], F32, R + 16 * K)
        zs = at("zs", [P, 8, SEQ], F32, R + 24 * K)
        xs = at("xs", [P, 16, SEQ], F32, R + 40 * K)
        ada_in0 = at("ada_in0", [P, 2, KT, ADA_W], F32, R + 72 * K)
        ada_acc0 = at("ada_acc0", [P, 2, 2, ADA_W], F32, R + 88 * K)
        ub0 = at("ub0", [P, 2, UB], F32, R + 92 * K)
        cacc0 = at("cacc0", [P, 2, SEQ], F32, R + 92 * K + 2 * UB * 4)
        wdt_f = at("wdt_f", [P, KT * 16], F32, H + 28 * K)
        sb_lr = at("sb_lr", [P, 2, 2, 1280], F32R, H)
        sb_l = at("sb_l", [P, 2, 1280], F32, H + 20 * K)
        sb_w = at("sb_w", [P, 2, 1280], F32, R + 88 * K)
        mix_sb = at("mix_sb", [P, 2, 4, SEQ], F32R, R + 72 * K)
        dts = at("dts", [P, 7, NT, 16], F32, R + 100 * K + 64)
        dt_raw, dt_l, dt_v, dt_a, dt_acs, dt_w = (dts[:, i] for i in range(6))
        acs = at("acs", [16, SEQ], F32, R + 98 * K)
        cb = at("cb", [P, 2, SEQ], F32, R + 88 * K)
        xdt = at("xdt", [P, NT, 256], F32, H + 2 * K)
        xw = at("xw", [P, 3, 256], F32, H + 6 * K)
        b_tok = at("b_tok", [P, 2, 3, P], F32, R + 92 * K)
        st = at("st", [P, 3, 256], F32, H + 11 * K)
        dm = at("dm", [P, 2, SEQ], F32, H + 14 * K)
        eb = at("eb", [P, 2, SEQ], F32, H + 18 * K)
        cs = at("cs", [P, 2, 384], F32, H + 22 * K)
        yt = at("yt", [P, SEQ], F32, H + 25 * K)
        acs_r = at("acs_r", [16, 2, SEQ], F32R, H + 27 * K)
        mix_ssm = at("mix_ssm", [P, 2, 8, SEQ], F32R, R + 40 * K)
        wdt = at("wdt", [P, 2, KT * 16 + P - 16], F32R, R + 102 * K)
        y_h = at("y_h", [P, KT, SEQ], F32, H)
        oneh = at("oneh", [33, 640], F32, R + 24 * K)
        relt = at("relt", [33, 16], F32, R + 27 * K)
        table = at("table", [16, 640], F32, R + 28 * K)

        act = at("act", [P, 2, FT, SEQ], F32R, R)
        ub = at("ub", [P, 4, UB], F32, R + 88 * K)
        cg = at("cg", [P, 2, SEQ], F32, R + 88 * K + 4 * UB * 4 + 64)
        cv = at("cv", [P, SEQ], F32, R + 92 * K + 4 * UB * 4 + 64)
        ada_in1 = at("ada_in1", [P, 2, KT, ADA_W], F32, H + 16 * K)
        ada_acc1 = at("ada_acc1", [P, 2, 2, ADA_W], F32, R + 100 * K)

        f1 = at("f1", [P, 16, SEQ], F32, R)
        v1 = at("v1", [P, NT, SEQ], F32, R + 32 * K)
        kcs = at("kcs", [P, 2, 4, SEQ], F32, R + 40 * K)
        fl_r = at("fl_r", [P, 2, 2, 16, 124], F32R, R + 56 * K)
        fl = at("fl", [P, 16, 124], F32, R + 88 * K)
        npar = at("npar", [P, NN], F32, R + 96 * K)
        wg_r = at("wg_r", [P, 2, KT * 48 + P - 48], F32R, R + 96 * K + -(-NN // 8) * 32)
        hid = at("hid", [P, 2, 2, 124], F32, R + 6 * K)
        kcmp = at("kcmp", [P, 124], F32, R + K)
        vcmp = at("vcmp", [31, 256], F32, R + 2 * K)
        gates = at("gates", [P, 48, NT], F32, R + 3 * K)
        gates_t = at("gates_t", [48, SEQ], F32, R + 4 * K)
        s_p = at("s_p", [P, 3, 1280], F32, R + 40 * K)
        p_t = at("p_t", [P, 2, 1280], F32, R + 55 * K)
        q_st = at("q_st", [P, 2, SEQ], F32, R + 65 * K)
        u_b = at("u_b", [P, 2, 2, SEQ], F32, R + 84 * K)
        mx = at("mx", [P, 3, NT], F32, R + 92 * K)
        rs = at("rs", [P, 3, NT], F32, R + 92 * K + 64)
        sc = at("sc", [P, 3, NT], F32, R + 92 * K + 128)
        mix1 = at("mix1", [P, 2, KT, SEQ], F32R, H)
        y_r = at("y_r", [P, KT, SEQ], F32, R + 16 * K)
        assert top[0] <= nc.sbuf_usable_end, (top[0], nc.sbuf_usable_end)

        ps = ctx.enter_context(nc.psum_tensor("ps", [P, 8, SEQ], F32))
        table_d = nc.dram_tensor("rel_table", (16, P, 640), F32)

        def sem(name):
            return ctx.enter_context(nc.semaphore(name))

        const_in, x_in = sem("const_in"), sem("x_in")
        landed = [sem("w_landed0"), sem("w_landed1")]
        w_hi, w_lo, pe_done, evac = sem("w_hi"), sem("w_lo"), sem("pe_done"), sem("evac")
        ada_landed = [sem("ada_landed0"), sem("ada_landed1")]
        ada_sum = [sem("ada_sum0"), sem("ada_sum1")]
        ada_mm, mod_ready = sem("ada_mm"), sem("mod_ready")
        cond_ready = sem("cond_ready")
        setup, table_mm, table_out, table_st = sem("setup"), sem("table_mm"), sem("table_out"), sem("table_st")
        n_sq, n_ss, n_rs, n_norm, n_dv, n_hi, n_lo = (
            sem(k) for k in ("n_sq", "n_ss", "n_rs", "n_norm", "n_dv", "n_hi", "n_lo"))
        y_sq, y_sum, res, res_odd = sem("y_sq"), sem("y_sum"), sem("res"), sem("res_odd")
        pad, conv, silu_x = sem("pad"), sem("conv"), sem("silu_x")
        dt_mm, dt_dv, dt_ac, dt_tr = (sem(k) for k in ("dt_mm", "dt_dv", "dt_ac", "dt_tr"))
        sb_z, sb_abs, sb_e, sb_L, sb_hi, sb_lo, sb_s, sb_wt, sb_pv, sb_mix = (
            sem(k) for k in ("sb_z", "sb_abs", "sb_e", "sb_L", "sb_hi", "sb_lo", "sb_s", "sb_wt", "sb_pv", "sb_mix"))
        g_pa, g_pe, g_ac, g_dv = sem("g_pa"), sem("g_pe"), sem("g_ac"), sem("g_dv")
        hd_bc, hd_e, hd_mask, hd_d, hd_x, hd_dv, hd_y = (
            sem(k) for k in ("hd_bc", "hd_e", "hd_mask", "hd_d", "hd_x", "hd_dv", "hd_y"))
        yg, ms_sq, ms_dv, ms_lo = sem("yg"), sem("ms_sq"), sem("ms_dv"), sem("ms_lo")
        f_dv, f_gelu = sem("f_dv"), sem("f_gelu")
        gt_w, gt_mm, gt_ac = sem("gt_w"), sem("gt_mm"), sem("gt_ac")
        npar_in, fl_dv, fl_hi, fl_lo, c_mm = (
            sem(k) for k in ("npar_in", "fl_dv", "fl_hi", "fl_lo", "c_mm"))
        shift_in = [sem("shift_in_k"), sem("shift_in_v")]
        u_in = [sem("u_in0"), sem("u_in1")]
        a_q, a_s, a_mx, a_neg, a_p, a_sc, a_n, a_t, a_pt, a_pv, a_hi, a_mix = (
            sem(k) for k in ("a_q", "a_s", "a_mx", "a_neg", "a_p", "a_sc", "a_n", "a_t", "a_pt", "a_pv", "a_hi",
                             "a_mix"))
        out_done = sem("out_done")

        def pc(name, i, rows=P):
            return par[0:rows, bass.ds(pcol[name][0] + i, 1)]

        def wait(e, s, value):
            if not isinstance(value, int) or value > 0:
                e.wait_ge(s, value)

        def product3(e, out, a, b, first, last):
            for n, (i, j) in enumerate(((0, 0), (0, 1), (1, 0))):
                mm = e.matmul(out, a[i], b[j], start=first and n == 0, stop=last and n == 2)
            return mm

        def a_col(i, k):
            return gains[:, 16 * i + k:16 * i + k + 1]

        def shift_col(i, k):
            c = 48 * (i // 2) + 24 * (i % 2) + k
            return modc[:, c:c + 1]

        def g_col(i, k):
            return gains[:, 16 * i + 8 + k:16 * i + 9 + k]

        def res_before(p, k):
            return 12 * p + 3 * (k // 2)

        def wait_residual(e, p, k):
            if k % 2:
                e.wait_ge(res_odd, 4 * p + k // 2 + 1)
            else:
                e.wait_ge(res, res_before(p, k) + 3)

        norms = [s_low, s_low, s_high, s_low]
        posts = [s_low, s_high, s_low, s_high]
        ys = [y_h, y_h, y_r, y_h]
        RS_IN, RS_SSM, RS_OUT = [0, 6, 10, 14], 2, [4, 8, 12, 16]
        SS_IN, SS_SSM, SS_OUT = [0, 10, 19, 28], 8, [9, 18, 27, 36]
        SQ_IN = [0, 8, 16, 24]

        SC_BEFORE = [7 * (u // 3) + 2 * (u % 3) for u in range(13)]
        T_BEFORE = [14 * (u // 6) + 7 * (u // 3 % 2) + 3 * (u % 3) for u in range(13)]

        def nsa_rows(u):
            if u % 3 < 2:
                return [(qt, (QOFF[qt], P * (qt + 1))) for qt in (3, 0, 2, 1)]
            return [(qt, (7 * qt + 4 * qt * (qt - 1), 7 + 8 * qt)) for qt in range(NT)]

        block = ctx.enter_context(nc.Block())

        @block.sync
        def _(sp):
            def load(name, i, s):
                ph = plan[name]
                src, first = weights[name]
                c = ph["c0"] + i
                wait(sp, w_lo, c - 1)
                sp.dma_start(raw[:, s, 0:ph["size"] * P], src[first + i]).then_inc(landed[s], 16)

            def load_ada(a, s, buf, nth):
                wait(sp, ada_sum[s], 9 * nth)
                sp.dma_start(buf[:, s], ada[a]).then_inc(ada_landed[s], 16)

            sp.dma_start(par[:, :], params).then_inc(const_in, 16)
            sp.dma_start(cf[:, :, :], consts[:, 0:4]).then_inc(const_in, 16)
            sp.dma_start(dm[:, 0:2, :].rearrange("p a b -> p (a b)")[:, 0:5 * P],
                         consts[:, 4:9].rearrange("p a b -> p (a b)")).then_inc(const_in, 16)
            sp.dma_start(wdt_f[:, :], w_dt).then_inc(const_in, 16)
            sp.dma_start(oneh[:, :], onehot).then_inc(const_in, 16)
            sp.dma_start(relt[0:REL_BUCKETS, :], relb).then_inc(const_in, 16)
            load_ada(0, 0, ada_in0, 0)
            load_ada(1, 1, ada_in0, 0)
            sp.dma_start(x[:, :, :], x_t.rearrange("(k p) t -> p k t", p=P)).then_inc(x_in, 16)
            load_ada(2, 0, ada_in0, 1)
            load_ada(3, 1, ada_in0, 1)
            for a in range(4, ADA_FIRST):
                load_ada(a, a % 2, ada_in0, a // 2)
            load("v0", 0, 0)
            load("v0", 1, 1)
            for name, ada_at in (("q", 8), ("k", 10), ("xbc", 12), ("z", 20)):
                n = plan[name]["n"] // 2
                if name == "xbc":
                    sp.wait_ge(table_out, 2)
                with sp.Fori(0, n) as t:
                    if name == "xbc":
                        sp.dma_start(table_d.ap()[:, bass.ds(32 * t, 32), :],
                                     table[:, :].unsqueeze(1).to_broadcast([16, 32, 640])).then_inc(table_st, 16)
                    for s in range(2):
                        load(name, 2 * t + s, s)
                        load_ada(2 * t + (ada_at + s), s, ada_in0, t + ada_at // 2)
            with sp.Fori(0, 4) as t:
                for s in range(2):
                    load("out0", 2 * t + s, s)
            with sp.Fori(0, 11) as t:
                for s in range(2):
                    load("up0", 2 * t + s, s)
            load("down0", 0, 0)
            load("down0", 1, 1)

            def down_loads(t, last=False):
                for a in range(6):
                    load_ada(6 * t + (24 + a), a % 2, ada_in1, 3 * t + (12 + a // 2))
                    if a in (0, 1, 3, 5):
                        i = (2, 3, 0, 4, 0, 5)[a]
                        if last and i >= 4:
                            load("v1", i - 4, i % 2)
                        else:
                            load("down0", 4 * t + i, i % 2)

            sp.wait_ge(pe_done, plan["down0"]["ev0"])
            with sp.Fori(0, 3) as t:
                down_loads(t)
            down_loads(3, last=True)
            sp.wait_ge(n_lo, 24)
            sp.dma_start(npar[:, :], nsa_params).then_inc(npar_in, 16)
            for i in range(4):
                load("f1", i, i % 2)
            for kv in range(2):
                sp.wait_ge(evac, plan["f1"]["t0"] + 2 * kv + 2)
                for g in range(NSA_GROUPS):
                    rows = f1[HD * (g % 2):HD * (g % 2) + HD, 2 * kv + g // 2, :]
                    sp.dma_start(kcs[0:HD, kv, g, :], rows).then_inc(shift_in[kv], 16)
                    sp.dma_start(kcs[HD:P, kv, g, 0:SEQ - 1], rows[:, 1:SEQ]).then_inc(shift_in[kv], 16)
            with sp.Fori(2, 4) as t:
                for s in range(2):
                    load("f1", 2 * t + s, s)
            load("w1", 0, 0)
            load("w1", 1, 1)
            load("w1", 2, 0)
            load("w1", 3, 1)
            load("out1", 0, 0)
            load("out1", 1, 1)
            sp.wait_ge(table_st, 64)
            sp.wait_ge(a_mix, 1)
            for pair in range(8):
                sp.wait_ge(a_mx, 24 * max(0, pair - 1) + 1)
                head = 8 * (pair // 4) + pair % 4
                src = bass.AP(table_d, head * P * 640 + P - 1, [[640 - 1, P], [4 * P * 640, 2], [1, SEQ]])
                sp.dma_start(u_b[:, pair % 2], src).then_inc(u_in[pair % 2], 16)
            load("out1", 2, 0)
            load("out1", 3, 1)
            with sp.Fori(0, 11) as t:
                for s in range(2):
                    load("up1", 2 * t + s, s)
            with sp.Fori(0, 8) as t:
                for s in range(2):
                    load("down1", 2 * t + s, s)
            for k in range(KT):
                wait_residual(sp, 3, k)
                sp.dma_start(out_t[k * P:(k + 1) * P, :], x[:, k, :]).then_inc(out_done, 16)
            sp.wait_ge(out_done, 16 * KT)

        @block.scalar
        def _(sa):
            def round_next(name, i, s):
                ph = plan[name]
                n = ph["size"] * P
                nth = ph["c0"] // 2 + (1 if s == 0 else 2)
                o_ = 1 - s
                sa.wait_ge(landed[o_], 16 * nth + (16 // 2) * (i - s))
                sa.wait_ge(pe_done, ph["ev0"] + ph["per"] * i)
                sa.copy(ring[:, o_, 0, 0:n], raw[:, o_, 0:n]).then_inc(w_hi, 1)

            def round_chunk(c, lo=0):
                sa.wait_ge(landed[c % 2], 16 * (c // 2 + 1))
                sa.copy(ring[:, c % 2, 0, lo:CW], raw[:, c % 2, lo:CW]).then_inc(w_hi, 1)

            def root(base, sums, s):
                sa.wait_ge(n_ss, sums)
                sa.activation(s["rstd"][:, :], ps[:, 6, :], ACT.Ln, bias=EPS).then_inc(n_rs, 1)
                sa.wait_ge(n_rs, base + 1)
                sa.activation(s["rstd"][:, :], s["rstd"][:, :], ACT.Exp, scale=-0.5).then_inc(n_rs, 1)

            def norm_in(i):
                s = norms[i]
                for k in range(KT):
                    if i == 0:
                        sa.wait_ge(x_in, 16)
                    else:
                        wait_residual(sa, i - 1, k)
                    if k >= 2:
                        sa.wait_ge(n_ss, SS_IN[i] + k - 1)
                    sa.activation(s["sq"][:, k % 2], x[:, k], ACT.Square).then_inc(n_sq, 1)
                root(RS_IN[i], SS_IN[i] + KT, s)
                for k in range(KT):
                    sa.wait_ge(n_dv, 8 * i + k + 1)
                    sa.copy(h[:, 0, k], s["hm"][:, k % HM]).then_inc(n_hi, 1)

            def evac_tile(name, x_, bank, out, func=ACT.Copy, **kw):
                sa.wait_ge(pe_done, plan[name]["ev0"] + 1 + x_)
                sa.activation(out, ps[:, bank, :], func, **kw).then_inc(evac, 1)

            def evac_copy(name, x_, bank, out):
                sa.wait_ge(pe_done, plan[name]["ev0"] + 1 + x_)
                sa.copy(out, ps[:, bank, :]).then_inc(evac, 1)

            def plain(name, out, first, func=ACT.Copy, **kw):
                with sa.Fori(0, plan[name]["n"] // 2) as t:
                    for s in range(2):
                        round_next(name, 2 * t + s, s)
                        for half in range(2):
                            x_ = 4 * t + (2 * s + half)
                            evac_tile(name, x_, 2 * s + half, out[:, bass.ds(x_ + first, 1), :], func, **kw)

            def tokens(name, i, v):
                ph = plan[name]
                c = ph["c0"]
                sa.wait_ge(pe_done, ph["ev0"] + 1)
                round_chunk(c + 2)
                for t in range(NT):
                    sa.wait_ge(pe_done, ph["ev0"] + 2 + t)
                    sa.copy(v[:, t], ps[:, t, :]).then_inc(evac, 1)

            def y_tile(p, name, x_, done, bank, par_):
                s = posts[p]
                sa.wait_ge(pe_done, done)
                sa.activation(ys[p][:, bass.ds(x_, 1), :], ps[:, bank:bank + 1, :], ACT.Copy).then_inc(y_sq, 1)
                wait(sa, y_sum, 9 * p + x_)
                sa.activation(s["sq"][:, par_], ps[:, bank, :], ACT.Square).then_inc(evac, 1)

            def root_out(p):
                root(RS_OUT[p], SS_OUT[p] + 1, posts[p])

            def ffn_up(l):
                name = f"up{l}"
                sa.preload_act_table(ACT.Gelu_apprx_tanh)
                with sa.Fori(0, FT // 2) as t:
                    for s in range(2):
                        round_next(name, 2 * t + s, s)
                        evac_copy(name, 4 * t + 2 * s, 2 * s, ub[:, 2 * s, PAD:])
                        sa.wait_ge(f_dv, 18 * t + (9 * FT * l + 9 * s + 3))
                        sa.activation(cg[:, s], cg[:, s], ACT.Gelu_apprx_tanh).then_inc(f_gelu, 1)
                        evac_copy(name, 4 * t + (2 * s + 1), 2 * s + 1, ub[:, 2 * s + 1, PAD:])

            def ffn_down(l):
                name = f"down{l}"
                ph = plan[name]
                sa.preload_act_table_set("natural_log_exp_and_others")

                def body(t, last=False):
                    for i in range(4):
                        if not (last and i == 3):
                            round_next4(name, t, i)
                        if i % 2:
                            y_tile(1 + 2 * l, name, 2 * t + i // 2, 4 * t + (ph["ev0"] + i + 1), i // 2, i // 2)

                def round_next4(name, t, i):
                    n = ph["size"] * P
                    o_ = (i + 1) % 2
                    c = ph["c0"] + i + 1
                    sa.wait_ge(landed[o_], 32 * t + 16 * (c // 2 + 1))
                    sa.wait_ge(pe_done, 4 * t + (ph["ev0"] + i))
                    sa.copy(ring[:, o_, 0, 0:n], raw[:, o_, 0:n]).then_inc(w_hi, 1)

                if l == 0:
                    with sa.Fori(0, 4) as t:
                        body(t)
                    round_chunk(plan["v1"]["c0"], 11 * P)
                else:
                    with sa.Fori(0, 3) as t:
                        body(t)
                    body(3, last=True)

            sa.wait_ge(const_in, 96)
            sa.activation(cond[:, :], par[:, pcol["cond"][0]:pcol["cond"][0] + KT], ACT.Silu).then_inc(cond_ready, 1)
            sa.preload_act_table_set("natural_log_exp_and_others")
            round_chunk(0)
            round_chunk(1)
            norm_in(0)
            tokens("v0", 0, v0)
            plain("q", qk0, 0, scale=HD ** -0.5)
            plain("k", qk0, 4)
            def convolved(x_, half):
                sa.wait_ge(conv, 4 * x_ + 4)
                sa.activation(xs[:, bass.ds(x_, 1), :], cacc0[:, half:half + 1, :], ACT.Silu).then_inc(silu_x, 1)

            def xbc(t, first=False):
                for s in range(2):
                    round_next("xbc", 2 * t + s, s)
                    for half in range(2):
                        n = 2 * s + half
                        evac_copy("xbc", 4 * t + n, n, ub0[:, n % 2, PAD:])
                        if n or not first:
                            convolved(4 * t + (n - 1), (n - 1) % 2)

            sa.preload_act_table(ACT.Silu)
            xbc(0, first=True)
            with sa.Fori(1, 4) as t:
                xbc(t)
            convolved(15, 1)
            sa.wait_ge(table_st, 64)
            plain("z", zs, 0, ACT.Silu)

            sa.wait_ge(pe_done, plan["out0"]["ev0"])
            round_chunk(plan["out0"]["c0"] + 1)

            sa.preload_act_table_set("natural_log_exp_and_others")
            sa.activation(dts[:, 6, 0, :], par[:, pcol["a_log"][0]:pcol["a_log"][0] + 16], ACT.Exp).then_inc(dt_ac, 1)
            sa.wait_ge(dt_dv, 3)
            sa.activation(dt_l, dt_l, ACT.Exp).then_inc(dt_ac, 1)
            sa.wait_ge(dt_ac, 2)
            sa.activation(dt_l, dt_l, ACT.Ln, bias=1.0).then_inc(dt_ac, 1)
            sa.wait_ge(dt_mm, 4)
            sa.wait_ge(dt_dv, 7)
            sa.activation(dt_w, ps[:, 7, 64:128].rearrange("p (t h) -> p t h", t=NT), ACT.Exp).then_inc(dt_ac, 1)

            def softplus(u):
                if u >= 2:
                    sa.wait_ge(sb_lo, u - 1)
                for n, (at_, w) in enumerate(BANKS):
                    sa.wait_ge(sb_z, 3 * u + n + 1)
                    sa.activation(sb_l[:, u % 2, at_:at_ + w], ps[:, 3 * (u % 2) + n, 0:w], ACT.Abs).then_inc(sb_abs, 1)
                sa.wait_ge(sb_abs, 3 * u + 3)
                sa.activation(sb_l[:, u % 2], sb_l[:, u % 2], ACT.Exp, scale=-1.0).then_inc(sb_e, 1)
                sa.wait_ge(sb_e, 2 * u + 1)
                sa.activation(sb_l[:, u % 2], sb_l[:, u % 2], ACT.Ln, bias=1.0).then_inc(sb_e, 1)

            softplus(0)
            softplus(1)
            for u in range(SB_HEADS):
                wait(sa, sb_pv, u - 1)
                for n, (at_, w) in enumerate(BANKS):
                    sa.wait_ge(sb_s, 3 * u + n + 1)
                    sa.activation(sb_w[:, u % 2, at_:at_ + w], ps[:, 3 * (u % 2) + n, 0:w], ACT.Exp).then_inc(sb_wt, 1)
                if u + 2 < SB_HEADS:
                    softplus(u + 2)

            def gated_squares(k):
                sa.wait_ge(yg, 3 * k + 2)
                sa.activation(s_low["sq"][:, k % 2], zs[:, k], ACT.Square).then_inc(ms_sq, 1)

            def group_copies(g):
                wait(sa, hd_dv, 16 * (g - 1))
                sa.wait_ge(g_pa, 2 * g + 1)
                sa.copy(cb[:, g % 2], ps[:, 0, :]).then_inc(g_ac, 1)
                sa.wait_ge(g_pa, 2 * g + 2)
                sa.copy(b_tok[:, g % 2], ps[:, 3, 0:384].rearrange("p (c n) -> p c n", c=3)).then_inc(g_ac, 1)

            def head_exp(n):
                sa.wait_ge(hd_bc, n + 1)
                wait(sa, hd_dv, 4 * (n - 1))
                sa.activation(eb[:, n % 2], ps[:, 6 + n % 2, :], ACT.Exp).then_inc(hd_e, 1)

            group_copies(0)
            head_exp(0)
            for g in range(SSM_GROUPS):
                wait(sa, hd_y, 4 * g)
                sa.wait_ge(g_pe, 3 * g + 3)
                sa.copy(st[:, 0, :], ps[:, 4, 0:256]).then_inc(g_ac, 1)
                for hh in range(4):
                    n = 4 * g + hh
                    if n + 1 < SSM_HEADS:
                        head_exp(n + 1)
                    if hh == 3:
                        gated_squares(2 * g)
                    sa.wait_ge(hd_d, n + 1)
                    sa.activation(dm[:, n % 2], dm[:, n % 2], ACT.Exp).then_inc(hd_x, 1)
                if g + 1 < SSM_GROUPS:
                    group_copies(g + 1)
                gated_squares(2 * g + 1)
            root(RS_SSM, SS_SSM + 1, s_low)

            def out0(t):
                for s in range(2):
                    if s or not isinstance(t, int):
                        round_next("out0", 2 * t + s, s)
                    y_tile(0, "out0", 2 * t + s, 2 * t + (plan["out0"]["ev0"] + s + 1), s, s)

            out0(0)
            with sa.Fori(1, 4) as t:
                out0(t)
            round_chunk(plan["up0"]["c0"], 12 * P)
            root_out(0)
            norm_in(1)
            ffn_up(0)
            ffn_down(0)
            sa.wait_ge(pe_done, plan["v1"]["ev0"])
            round_chunk(plan["v1"]["c0"] + 1)
            root_out(1)

            norm_in(2)
            tokens("v1", 2, v1)

            def f1_tiles(t, **kw):
                for s in range(2):
                    round_next("f1", 2 * t + s, s)
                    for half in range(2):
                        x_ = 4 * t + (2 * s + half)
                        evac_tile("f1", x_, 2 * s + half, f1[:, bass.ds(x_, 1), :], **kw)

            def blocks_high(kv):
                sa.wait_ge(fl_dv, 16 * kv + 16)
                sa.copy(fl_r[:, kv, 0], fl[:, :, :]).then_inc(fl_hi, 1)

            f1_tiles(0)
            f1_tiles(1, scale=HD ** -0.5)
            blocks_high(0)
            f1_tiles(2, scale=HD ** -0.5)
            blocks_high(1)
            f1_tiles(3)
            for kv in range(2):
                for part in range(2):
                    round_next("w1", 2 * kv + part, part)
                sa.wait_ge(pe_done, plan["w1"]["ev0"] + 2 * kv + 2)
                for hh in range(2):
                    col = ncol["b1"][0] + 2 * kv + hh
                    sa.activation(hid[:, kv, hh], ps[:, 2 * kv + hh, 0:124], ACT.Silu,
                                  bias=npar[:, col:col + 1]).then_inc(evac, 1)
                if kv == 0:
                    sa.wait_ge(gt_mm, 1)
                    sa.copy(gates_t[:, :], ps[0:48, 6, :]).then_inc(gt_ac, 1)
            sa.preload_act_table_set("natural_log_exp_and_others")
            sa.wait_ge(gt_mm, 2)
            sa.activation(gates[:, :, :].rearrange("p c t -> p t c"),
                          ps[:, 7, 0:192].rearrange("p (t c) -> p t c", t=NT), ACT.Exp, scale=-1.0).then_inc(a_pt, 1)

            def nsa_exp(gp, t, u):
                r = u % 3
                sa.wait_ge(a_neg, 12 * t + (24 * gp + u + 1))
                for qt, (at_, w) in nsa_rows(u):
                    sa.activation(s_p[:, r, at_:at_ + w], s_p[:, r, at_:at_ + w], ACT.Exp,
                                  bias=mx[:, r, qt:qt + 1], accum_out=rs[:, r, qt:qt + 1]).then_inc(a_p, 1)

            def nsa_high(gp, t, pr):
                sa.wait_ge(a_pv, 12 * t + (24 * gp + 6 * pr + 7))
                j = 2 * t + (4 * gp + pr)
                sa.activation(mix1[:, 0, bass.ds(j, 1), :], ps[:, 6 + pr:7 + pr, :], ACT.Copy).then_inc(a_hi, 1)

            def nsa_take(gp, t, u):
                sa.wait_ge(a_pv, 12 * t + (24 * gp + max(0, u - 1) + 1))
                for n, (at_, w) in enumerate(BANKS[:3 if u % 3 < 2 else 1]):
                    rows = P if u % 3 < 2 else CMP_N
                    sa.wait_ge(a_t, 28 * t + (56 * gp + T_BEFORE[u] + n + 2))
                    sa.copy(p_t[0:rows, u % 2, at_:at_ + w], ps[0:rows, 3 + n, 0:w]).then_inc(a_pt, 1)

            for gp in range(2):
                with sa.Fori(0, 2) as t:
                    for v in range(15):
                        if v < 12:
                            nsa_exp(gp, t, v)
                        if 2 <= v < 14:
                            nsa_take(gp, t, v - 2)
                        if v in (9, 14):
                            nsa_high(gp, t, v // 14)
            sa.preload_act_table_set("natural_log_exp_and_others")
            with sa.Fori(0, 2) as t:
                for s in range(2):
                    round_next("out1", 2 * t + s, s)
                    for half in range(2):
                        x_ = 4 * t + (2 * s + half)
                        y_tile(2, "out1", x_, 4 * t + (plan["out1"]["ev0"] + 2 * s + half + 1), 2 * s + half, half)
            root_out(2)
            norm_in(3)
            ffn_up(1)
            ffn_down(1)
            root_out(3)

        @block.gpsimd
        def _(gp_):
            def lower(name, first=0, last=None):
                ph = plan[name]
                n = ph["size"] * P
                last = ph["n"] if last is None else last

                def body(i, s):
                    gp_.wait_ge(w_hi, i + (ph["c0"] + 1 + ph["extra"]))
                    gp_.tensor_tensor(ring[:, s, 1, 0:n], raw[:, s, 0:n], ring[:, s, 0, 0:n].bitcast(F32),
                                      ALU.subtract).then_inc(w_lo, 1)
                if last - first <= 2:
                    for i in range(first, last):
                        body(i, i % 2)
                    return
                if first % 2:
                    body(first, 1)
                with gp_.Fori((first + 1) // 2, last // 2) as t:
                    for s in range(2):
                        body(2 * t + s, s)

            def residual(p):
                for k in range(1, KT, 2):
                    gp_.wait_ge(res, res_before(p, k - 1) + 1)
                    gp_.tensor_tensor(x[:, k], x[:, k], ys[p][:, k], ALU.add).then_inc(res_odd, 1)

            def norm_in(i):
                s = norms[i]
                for k in range(KT):
                    gp_.wait_ge(n_hi, SQ_IN[i] + k + 1)
                    gp_.tensor_tensor(h[:, 1, k], s["hm"][:, k % HM], h[:, 0, k].bitcast(F32),
                                      ALU.subtract).then_inc(n_lo, 1)

            lower("v0", 0, 1)
            norm_in(0)
            lower("v0", 1)
            for name in ("q", "k", "xbc", "z"):
                lower(name)
            lower("out0", 0, 2)
            for u in range(SB_HEADS):
                gp_.wait_ge(sb_hi, u + 1)
                gp_.tensor_tensor(sb_lr[:, u % 2, 1], sb_l[:, u % 2], sb_lr[:, u % 2, 0].bitcast(F32),
                                  ALU.subtract).then_inc(sb_lo, 1)
            for k in range(8):
                gp_.wait_ge(ms_dv, 2 * k + 2)
                gp_.tensor_tensor(mix_ssm[:, 1, k], s_low["hm"][:, k % HM], mix_ssm[:, 0, k].bitcast(F32),
                                  ALU.subtract).then_inc(ms_lo, 1)
            lower("out0", 2)
            lower("up0", 0, 1)
            residual(0)
            norm_in(1)
            lower("up0", 1)
            lower("down0")
            lower("v1", 0, 1)
            residual(1)
            norm_in(2)
            lower("v1", 1)

            def blocks_low(kv):
                gp_.wait_ge(fl_hi, kv + 1)
                gp_.tensor_tensor(fl_r[:, kv, 1], fl[:, :, :], fl_r[:, kv, 0].bitcast(F32),
                                  ALU.subtract).then_inc(fl_lo, 1)

            lower("f1", 0, 4)
            lower("f1", 4, 5)
            blocks_low(0)
            lower("f1", 5, 7)
            blocks_low(1)
            lower("f1", 7)
            gp_.wait_ge(w_lo, plan["out1"]["c0"])
            lower("out1")
            lower("up1", 0, 1)
            residual(2)
            norm_in(3)
            lower("up1", 1)
            lower("down1")
            residual(3)

        @block.tensor
        def _(pe):
            def weights_of(s, j):
                return ring[:, s, 0, j * P:(j + 1) * P], ring[:, s, 1, j * P:(j + 1) * P]

            def split(tensor, k):
                return tensor[:, 0, k], tensor[:, 1, k]

            def norm_sums(i):
                wait(pe, n_rs, RS_IN[i])
                for k in range(KT):
                    pe.wait_ge(n_sq, SQ_IN[i] + k + 1)
                    pe.matmul(ps[:, 6, :], mean_of, norms[i]["sq"][:, k % 2], start=k == 0, stop=k == KT - 1).then_inc(n_ss, 1)

            def out_sums(p):
                pe.wait_ge(y_sum, 9 * p + 9)
                pe.matmul(ps[:, 6, :], mean_of, posts[p]["ssum"][:, :], start=True, stop=True).then_inc(n_ss, 1)

            def tokens(name, i):
                ph = plan[name]
                wait(pe, evac, ph["t0"])
                for part in range(2):
                    pe.wait_ge(w_lo, ph["c0"] + part + 1)
                    for n in range(16):
                        k, t = (n // 4, n % 4) if part == 0 else (n % 4, n // 4)
                        kk = 4 * part + k
                        if n < 4 if part else n % 4 == 0:
                            pe.wait_ge(n_lo, 8 * i + kk + 1)
                        hs = tuple(a[:, t * P:(t + 1) * P] for a in split(h, kk))
                        w = tuple(ring[:, part, j, k * SEQ:(k + 1) * SEQ] for j in range(2))
                        mm = product3(pe, ps[:, t, :], hs, w, kk == 0, kk == KT - 1)
                        if (part == 0 and n == 15) or (part == 1 and k == 3):
                            mm.then_inc(pe_done, 1)

            def features(name, i, s, rhs, banks=(0, 1, 2, 3), free=3):
                ph = plan[name]
                pe.wait_ge(w_lo, i + (ph["c0"] + 1))
                for half in range(2):
                    pe.wait_ge(evac, 2 * i + (ph["t0"] + half - free))
                    for k in range(KT):
                        mm = product3(pe, ps[:, banks[2 * s + half], :], weights_of(s, 8 * half + k), split(rhs, k),
                                      k == 0, k == KT - 1)
                    mm.then_inc(pe_done, 1)

            def first_features(name, i):
                ph = plan[name]
                pe.wait_ge(w_lo, ph["c0"] + 1)
                pe.wait_ge(evac, ph["t0"])
                for k in range(KT):
                    pe.wait_ge(n_lo, 8 * i + k + 1)
                    for half in range(2):
                        mm = product3(pe, ps[:, half, :], weights_of(0, 8 * half + k), split(h, k), k == 0, k == KT - 1)
                        if k == KT - 1:
                            mm.then_inc(pe_done, 1)

            def ada_sum_up(a, s, acc, nth):
                pe.wait_ge(ada_sum[s], 9 * nth + 9)
                for half in range(2):
                    mm = pe.matmul(ps[:, 7, bass.ds(2 * a + half, 1)], acc[:, s, 0, half * P:(half + 1) * P], one[:, :],
                                   start=True, stop=True)
                mm.then_inc(ada_mm, 1)

            def feature_phase(name, ada_at=None, first=0):
                with pe.Fori(first, plan[name]["n"] // 2) as t:
                    for s in range(2):
                        features(name, 2 * t + s, s, h)
                        if ada_at is not None:
                            a = ada_at - 1 + s
                            ada_sum_up(2 * t + a, a % 2, ada_acc0, t + a // 2)

            pe.wait_ge(const_in, 96)
            pe.wait_ge(setup, 2)
            for n in range(2):
                pe.matmul(ps[0:16, n, 0:320], relt[:, :], oneh[:, 320 * n:320 * n + 320],
                          start=True, stop=True).then_inc(table_mm, 1)
            for a in range(ADA_FIRST):
                ada_sum_up(a, a % 2, ada_acc0, a // 2)
            norm_sums(0)
            pe.wait_ge(table_out, 2)
            tokens("v0", 0)
            features("q", 0, 0, h)
            features("q", 1, 1, h)
            ada_sum_up(8, 0, ada_acc0, 4)
            feature_phase("k", 10)
            feature_phase("xbc", 12)
            feature_phase("z", 20)
            ada_sum_up(23, 1, ada_acc0, 11)

            pe.wait_ge(setup, 6)
            for k in range(KT):
                w = tuple(wdt[:, j, 16 * k:16 * k + P] for j in range(2))
                mm = product3(pe, ps[:, 6, :], w, split(h, k), k == 0, k == KT - 1)
            mm.then_inc(dt_mm, 1)

            def sb_scores(u):
                b, i, bank = u % 2, u // 2, 3 * (u % 2)
                if u < 2:
                    pe.wait_ge(evac, plan["out0"]["t0"])
                else:
                    pe.wait_ge(sb_wt, 3 * (u - 1))
                rows = slice(HD * b, HD * b + HD)
                for n, tiles in enumerate(((0,), (1, 3), (2,))):
                    for kt in tiles:
                        off = KOFF[kt] - SEQ * n
                        mm = pe.matmul(ps[:, bank + n, off:off + SEQ - P * kt], qk0[rows, 4 + i, P * kt:P * kt + P],
                                       qk0[rows, i, P * kt:], start=kt == tiles[0], stop=False, skip_group_check=True)
                        mm = pe.matmul(ps[:, bank + n, off:off + P], ident_r, mask_sb,
                                       start=False, stop=False, skip_group_check=True)
                    mm.then_inc(sb_z, 1)

            def sb_suffix(u):
                bank = 3 * (u % 2)
                pe.wait_ge(sb_lo, u + 1)
                for n, tiles in enumerate(((0,), (1, 3), (2,))):
                    for kt in tiles:
                        for k2 in range(kt, NT):
                            w = SEQ - P * k2
                            off = KOFF[kt] - SEQ * n + P * (k2 - kt)
                            for part in range(2):
                                mm = pe.matmul(ps[:, bank + n, off:off + w], neg_suffix if k2 == kt else neg_ones,
                                               sb_lr[:, u % 2, part, KOFF[k2]:KOFF[k2] + w], start=False,
                                               stop=False, skip_group_check=True)
                    mm.then_inc(sb_s, 1)

            def sb_values(u):
                b, i = u % 2, u // 2
                pe.wait_ge(sb_wt, 3 * u + 3)
                if u % 2 == 0 and u >= 4:
                    pe.wait_ge(sb_mix, 2 * (i - 1))
                for kt in range(NT):
                    mm = pe.matmul(ps[HD * b:HD * b + HD, 6 + i % 2, P * kt:], v0[:, kt, HD * u:HD * u + HD],
                                   sb_w[:, u % 2, KOFF[kt]:KOFF[kt] + SEQ - P * kt], start=kt == 0, stop=kt == NT - 1,
                                   skip_group_check=True)
                mm.then_inc(sb_pv, 1)

            sb_scores(0)
            pe.wait_ge(dt_dv, 1)
            for t in range(NT):
                mm = pe.transpose(ps[:, 6, 16 * t:16 * t + 16], acs[:, P * t:P * t + P], ident[0:16, 0:16])
            mm.then_inc(dt_mm, 1)
            pe.wait_ge(dt_dv, 6)
            pe.wait_ge(mod_ready, 3)
            for n, tri in enumerate((tri_le, tri_gt)):
                pe.matmul(ps[:, 7, 64 * n:64 * n + 64], tri, dt_a.rearrange("p t h -> p (t h)"),
                          start=True, stop=True).then_inc(dt_mm, 1)
            sb_scores(1)
            pe.wait_ge(dt_dv, 7)
            for t in range(NT):
                mm = pe.transpose(ps[0:16, 6, P * t:P * t + P], dt_acs[:, t, :], ident)
            mm.then_inc(dt_tr, 1)
            pe.wait_ge(dt_dv, 9)
            for u in range(SB_HEADS):
                sb_suffix(u)
                if u >= 1:
                    sb_values(u - 1)
                if u + 2 < SB_HEADS:
                    sb_scores(u + 2)
            sb_values(SB_HEADS - 1)

            def group_ahead(g):
                wait(pe, g_ac, 3 * g - 1)
                for c in range(NT):
                    mm = pe.matmul(ps[:, 0, P * c:P * c + P], xs[:, 8 + g, P * c:P * c + P], xs[:, 12 + g, P * c:P * c + P],
                                   start=True, stop=True)
                mm.then_inc(g_pa, 1)
                for c in range(3):
                    mm = pe.transpose(ps[:, 3, P * c:P * c + P], xs[:, 8 + g, P * c:P * c + P], ident)
                mm.then_inc(g_pa, 1)

            def head_decays(n):
                wait(pe, hd_d, n - 1)
                for j in range(2):
                    mm = pe.matmul(ps[:, 6 + n % 2, :], ident_r[0:16, n:n + 1].to_broadcast([16, P]), acs_r[:, j],
                                   start=j == 0, stop=False, skip_group_check=True)
                mm.then_inc(hd_bc, 1)

            pe.wait_ge(sb_mix, 8)
            pe.wait_ge(dt_dv, 11)
            group_ahead(0)
            head_decays(0)
            for g in range(SSM_GROUPS):
                wait(pe, yg, 6 * g - 2)
                for n in range(2):
                    for j in range(2):
                        for f in range(2):
                            c = 2 * n + j
                            mm = pe.transpose(ps[:, 1 + n, 256 * j + P * f:256 * j + P * f + P],
                                              xs[:, 2 * g + f, P * c:P * c + P], ident)
                    mm.then_inc(g_pe, 1)
                pe.wait_ge(g_ac, 3 * g + 2)
                pe.wait_ge(g_dv, 4 * g + 4)
                wait(pe, hd_dv, 16 * g)
                for c in range(3):
                    mm = pe.matmul(ps[:, 4 + c // 2, 256 * (c % 2):256 * (c % 2) + 256], b_tok[:, g % 2, c], xw[:, c],
                                   start=True, stop=True)
                mm.then_inc(g_pe, 1)

                def head_y(n):
                    hh = n % 4
                    b = hh % 2
                    pe.wait_ge(hd_dv, 4 * n + 4)
                    out = ps[HD * b:HD * b + HD, 1 + hh // 2, :]
                    for c in range(NT):
                        mm = pe.matmul(out[:, P * c:P * c + P], xdt[:, c, HD * hh:HD * hh + HD],
                                       dm[:, n % 2, P * c:P * c + P], start=c == 0, stop=False, skip_group_check=True)
                    for c in range(1, NT):
                        mm = pe.matmul(out[:, P * c:P * c + P], st[:, c - 1, HD * hh:HD * hh + HD],
                                       cs[:, n % 2, P * (c - 1):P * c], start=False, stop=c == NT - 1,
                                       skip_group_check=True)
                    mm.then_inc(hd_y, 1)

                for hh in range(4):
                    n = 4 * g + hh
                    if n + 1 < SSM_HEADS:
                        head_decays(n + 1)
                    pe.wait_ge(hd_e, n + 1)
                    pe.matmul(ps[:, 6 + n % 2, :].rearrange("p (c l) -> p c l", c=NT), ident_r,
                              mask_ssd.unsqueeze(1).to_broadcast([P, NT, P]), start=False, stop=True,
                              skip_group_check=True).then_inc(hd_mask, 1)
                    if hh:
                        head_y(n - 1)
                    if hh == 2 and g + 1 < SSM_GROUPS:
                        group_ahead(g + 1)
                head_y(4 * g + 3)

            def mixed(k):
                return split(mix_sb, k) if k < 4 else split(mix_ssm, k - 4)

            def first_two(ks):
                for k in ks:
                    if k >= 4:
                        pe.wait_ge(ms_lo, k - 3)
                    for s in range(2):
                        mm = product3(pe, ps[:, s, :], weights_of(s, k), mixed(k), k == 0, k == 11)
                        if k == 11:
                            mm.then_inc(pe_done, 1)

            ph = plan["out0"]
            pe.wait_ge(w_lo, ph["c0"] + 2)
            pe.wait_ge(evac, ph["t0"])
            pe.wait_ge(yg, 19)
            first_two(range(4))
            pe.wait_ge(yg, 24)
            pe.matmul(ps[:, 6, :], mean_of, s_low["ssum"][:, :], start=True, stop=True).then_inc(n_ss, 1)
            first_two(range(4, 12))
            with pe.Fori(1, 4) as t:
                for s in range(2):
                    pe.wait_ge(w_lo, 2 * t + (ph["c0"] + s + 1))
                    pe.wait_ge(evac, 2 * t + (ph["t0"] + s - 1))
                    for k in range(12):
                        mm = product3(pe, ps[:, s, :], weights_of(s, k), mixed(k), k == 0, k == 11)
                    mm.then_inc(pe_done, 1)
            out_sums(0)

            def ffn(l):
                i = 1 + 2 * l
                norm_sums(i)
                first_features(f"up{l}", i)
                features(f"up{l}", 1, 1, h)
                feature_phase(f"up{l}", first=1)
                ph = plan[f"down{l}"]

                def body(t):
                    for c in range(4):
                        pe.wait_ge(w_lo, 4 * t + (ph["c0"] + c + 1))
                        if isinstance(t, int) and c < 2:
                            pe.wait_ge(evac, ph["t0"] - 3)
                            pe.wait_ge(f_dv, 9 * (FT * l + 11 * (c + 1)))
                        elif c % 2 == 0:
                            pe.wait_ge(evac, 2 * t + (ph["t0"] + c // 2 - 1))
                        for j in range(11):
                            k = 11 * (c % 2) + j
                            mm = product3(pe, ps[:, c // 2, :], weights_of(c % 2, j), split(act, k), k == 0, k == FT - 1)
                        mm.then_inc(pe_done, 1)
                        if l == 0:
                            for a in ((-1,), (0, 1), (2,), (3, 4))[c]:
                                if a >= 0 or not isinstance(t, int):
                                    ada_sum_up(6 * t + (24 + a), a % 2, ada_acc1, 3 * t + (12 + a // 2))

                body(0)
                with pe.Fori(1, 4) as t:
                    body(t)
                if l == 0:
                    ada_sum_up(47, 1, ada_acc1, 23)
                out_sums(1 + 2 * l)

            ffn(0)

            norm_sums(2)
            tokens("v1", 2)
            feature_phase("f1")
            for kv in range(2):
                for part in range(2):
                    ph = plan["w1"]
                    pe.wait_ge(w_lo, ph["c0"] + 2 * kv + part + 1)
                    pe.wait_ge(fl_lo, kv + 1)
                    pe.wait_ge(evac, ph["t0"])
                    for i in range(8):
                        for hh in range(2):
                            mm = product3(pe, ps[:, 2 * kv + hh, 0:124], weights_of(part, 2 * i + hh),
                                          tuple(fl_r[:, kv, j, 8 * part + i] for j in range(2)),
                                          part == 0 and i == 0, part == 1 and i == 7)
                    mm.then_inc(pe_done, 1)
                if kv == 0:
                    pe.wait_ge(gt_w, 3)
                    for k in range(KT):
                        w = tuple(wg_r[:, j, 48 * k:48 * k + P] for j in range(2))
                        mm = product3(pe, ps[:, 6, :], w, split(h, k), k == 0, k == KT - 1)
                    mm.then_inc(gt_mm, 1)
            pe.wait_ge(gt_ac, 1)
            for t, signal in enumerate((a_s, a_t, a_pv, gt_mm)):
                pe.transpose(ps[:, 7, 48 * t:48 * t + 48], gates_t[:, P * t:P * t + P],
                             ident[0:48, 0:48]).then_inc(signal, 1)
            pe.wait_ge(evac, plan["w1"]["t0"] + 2)
            c0 = ncol["w2k"][0]
            for hh in range(2):
                mm = pe.matmul(ps[:, 4, 0:124], npar[:, c0 + P * hh:c0 + P * hh + P], hid[:, 0, hh],
                               start=hh == 0, stop=hh == 1)
            mm.then_inc(c_mm, 1)
            pe.wait_ge(evac, plan["w1"]["t0"] + 4)
            c0 = ncol["w2v"][0]
            for g in range(NSA_GROUPS):
                for hh in range(2):
                    mm = pe.matmul(ps[0:CMP_N, 5, HD * g:HD * g + HD], hid[:, 1, hh, CMP_N * g:CMP_N * g + CMP_N],
                                   npar[:, c0 + HD * hh:c0 + HD * hh + HD], start=hh == 0, stop=hh == 1)
            mm.then_inc(c_mm, 1)
            def nsa_scores(gp, t, u):
                pr, b, br = u // 6, u // 3 % 2, u % 3
                g = 2 * gp + b
                rows = slice(HD * b, HD * b + HD)
                pe.wait_ge(a_q, 2 * t + (4 * gp + pr + 1))
                pe.wait_ge(a_mx, 48 * t + (96 * gp + 4 * u + 1))
                for n, qts in enumerate(((3,), (0, 2), (1,)) if br < 2 else ((0, 1, 2, 3),)):
                    for qt in qts:
                        at_, w = dict(nsa_rows(u))[qt]
                        keys = f1[rows, 12 + 2 * br + gp, 0:w] if br < 2 else kcmp[rows, CMP_N * g:CMP_N * g + w]
                        mm = pe.matmul(ps[:, n, at_ - BANKS[n][0]:at_ - BANKS[n][0] + w],
                                       q_st[rows, pr, P * qt:P * qt + P], keys, start=True, stop=True,
                                       skip_group_check=True)
                    mm.then_inc(a_s, 1)

            def nsa_turn(gp, t, u):
                pe.wait_ge(a_n, 48 * t + (96 * gp + 4 * u + 4))
                pe.wait_ge(a_pt, 28 * t + (56 * gp + T_BEFORE[u] + 1))
                r = u % 3
                if u % 3 < 2:
                    for n, tiles in enumerate(((0,), (1, 3), (2,))):
                        for kt in tiles:
                            for qt in range(kt, NT):
                                off = KOFF[kt] - BANKS[n][0] + P * (qt - kt)
                                mm = pe.transpose(ps[:, 3 + n, off:off + P],
                                                  s_p[:, r, QOFF[qt] + P * kt:QOFF[qt] + P * kt + P], ident)
                        mm.then_inc(a_t, 1)
                else:
                    for qt, (at_, w) in nsa_rows(u):
                        mm = pe.transpose(ps[0:w, 3, P * qt:P * qt + P], s_p[:, r, at_:at_ + w], ident)
                    mm.then_inc(a_t, 1)

            def nsa_values(gp, t, u):
                pr, b, br = u // 6, u // 3 % 2, u % 3
                g = 2 * gp + b
                pe.wait_ge(a_pt, 28 * t + (56 * gp + T_BEFORE[u + 1] + 1))
                if u % 6 == 0:
                    pe.wait_ge(a_mix, 2 * t + (4 * gp + pr + 2))
                out = ps[HD * b:HD * b + HD, 6 + pr, :]
                if br < 2:
                    for kt in range(NT):
                        c0 = 256 * br + HD * g
                        mm = pe.matmul(out[:, P * kt:], v1[:, kt, c0:c0 + HD],
                                       p_t[:, u % 2, KOFF[kt]:KOFF[kt] + SEQ - P * kt],
                                       start=br == 0 and kt == 0, stop=False, skip_group_check=True)
                else:
                    for qt, (at_, w) in nsa_rows(u):
                        mm = pe.matmul(out[:, P * qt:P * qt + P], vcmp[0:w, HD * g:HD * g + HD],
                                       p_t[0:w, u % 2, P * qt:P * qt + P], start=False, stop=qt == NT - 1,
                                       skip_group_check=True)
                mm.then_inc(a_pv, 1)

            for gp in range(2):
                with pe.Fori(0, 2) as t:
                    for v in range(15):
                        if v < 12:
                            nsa_scores(gp, t, v)
                        if 2 <= v < 14:
                            nsa_turn(gp, t, v - 2)
                        if v >= 3:
                            nsa_values(gp, t, v - 3)

            pe.wait_ge(a_mix, 11)
            with pe.Fori(0, 2) as t:
                for s in range(2):
                    features("out1", 2 * t + s, s, mix1)
            out_sums(2)
            ffn(1)

        @block.vector
        def _(ve):
            def ada_step(k, a, s, buf, acc, nth):
                if k == 0:
                    ve.wait_ge(ada_landed[s], 16 * nth + 16)
                    wait(ve, ada_mm, a - 1)
                if k < 2:
                    ve.tensor_scalar(acc[:, s, k], buf[:, s, k], cond[:, k:k + 1], None, ALU.mult).then_inc(ada_sum[s], 1)
                elif k < KT:
                    ve.wait_ge(ada_sum[s], 9 * nth + (k - 1))
                    ve.scalar_tensor_tensor(acc[:, s, k % 2], buf[:, s, k], cond[:, k:k + 1], acc[:, s, k % 2],
                                            ALU.mult, ALU.add).then_inc(ada_sum[s], 1)
                else:
                    ve.wait_ge(ada_sum[s], 9 * nth + KT)
                    ve.tensor_tensor(acc[:, s, 0], acc[:, s, 0], acc[:, s, 1], ALU.add).then_inc(ada_sum[s], 1)

            def ada_chunk(a, s, buf, acc, nth):
                for k in range(KT + 1):
                    ada_step(k, a, s, buf, acc, nth)

            def modulation(lo, hi):
                ve.wait_ge(ada_mm, hi // 2)
                ve.tensor_tensor(modc[:, lo:hi], ps[:, 7, lo:hi], par[:, pcol["ada_b"][0] + lo:pcol["ada_b"][0] + hi],
                                 ALU.add).then_inc(mod_ready, 1)

            def a_gain(i):
                c = 48 * (i // 2) + 24 * (i % 2) + 8
                g = pcol["norm_g"][0] + 16 * i
                ve.scalar_tensor_tensor(gains[:, 16 * i:16 * i + 8], modc[:, c:c + 8], 1.0, par[:, g:g + 8],
                                        ALU.add, ALU.mult).then_inc(mod_ready, 1)

            def g_gain(i):
                c = 48 * (i // 2) + 24 * (i % 2) + 16
                g = pcol["norm_g"][0] + 16 * i + 8
                ve.tensor_tensor(gains[:, 16 * i + 8:16 * i + 16], modc[:, c:c + 8], par[:, g:g + 8],
                                 ALU.mult).then_inc(mod_ready, 1)

            def norm_in(i):
                s = norms[i]
                ve.wait_ge(n_rs, RS_IN[i] + 2)
                def normalised(k):
                    if k >= HM:
                        ve.wait_ge(n_lo, 8 * i + k + 1 - HM)
                    if i and k % 2:
                        wait_residual(ve, i - 1, k)
                    ve.tensor_tensor(s["hm"][:, k % HM], x[:, k], s["rstd"][:, :], ALU.mult).then_inc(n_norm, 1)

                normalised(0)
                for k in range(KT):
                    if k + 1 < KT:
                        normalised(k + 1)
                    ve.wait_ge(n_norm, 8 * i + k + 1)
                    ve.tensor_scalar(s["hm"][:, k % HM], s["hm"][:, k % HM], a_col(i, k), shift_col(i, k),
                                     ALU.mult, ALU.add).then_inc(n_dv, 1)

            def y_start(p):
                ve.memset(posts[p]["ssum"][:, :], 0.0).then_inc(y_sum, 1)

            def y_square(p, tile0, x_, par_):
                s = posts[p]
                ve.wait_ge(evac, x_ + (tile0 + 1))
                ve.wait_ge(y_sum, x_ + (9 * p + 1))
                ve.tensor_tensor(s["ssum"][:, :], s["ssum"][:, :], s["sq"][:, par_], ALU.add).then_inc(y_sum, 1)

            def residual(p):
                s, y = posts[p], ys[p]
                ve.wait_ge(n_rs, RS_OUT[p] + 2)
                for k in range(0, KT, 2):
                    for j in (k + 1, k):
                        ve.scalar_tensor_tensor(y[:, j], y[:, j], g_col(p, j), s["rstd"][:, :],
                                                ALU.mult, ALU.mult).then_inc(res, 1)
                    ve.wait_ge(res, res_before(p, k) + 2)
                    ve.tensor_tensor(x[:, k], x[:, k], y[:, k], ALU.add).then_inc(res, 1)

            def taps(out, src, w_col, b_col, width, done, at_, between=lambda j: None):
                first = PAD - width + 1
                ve.tensor_scalar(out, src[:, first + width - 1:first + width - 1 + SEQ], w_col(width - 1), b_col,
                                 ALU.mult, ALU.add).then_inc(done, 1)
                between(0)
                for j in range(width - 2, -1, -1):
                    ve.wait_ge(done, at_ + (width - 1 - j))
                    ve.scalar_tensor_tensor(out, src[:, first + j:first + j + SEQ], w_col(j), out,
                                            ALU.mult, ALU.add).then_inc(done, 1)
                    between(width - 1 - j)

            def ffn(l):
                name = f"up{l}"
                for n in range(4):
                    ve.memset(ub[:, n, 0:PAD], 0.0).then_inc(pad, 1)
                ve.wait_ge(pad, 4 * l + 6)
                with ve.Fori(0, FT // 2) as t:
                    for s in range(2):
                        base = 18 * t + (9 * FT * l + 9 * s)
                        for half, out in ((0, cg[:, s]), (1, cv[:, :])):
                            ve.wait_ge(evac, 4 * t + (plan[name]["t0"] + 2 * s + half + 1))
                            i = 2 * t + (s + FT * half)
                            taps(out, ub[:, 2 * s + half], lambda j: pc(f"fconv_w{l}", 3 * i + j),
                                 pc(f"fconv_b{l}", i), 3, f_dv, base + 3 * half)
                        ve.wait_ge(f_gelu, 2 * t + (FT * l + s + 1))
                        ve.wait_ge(f_dv, base + 6)
                        ve.tensor_tensor(cv[:, :], cg[:, s], cv[:, :], ALU.mult).then_inc(f_dv, 1)
                        ve.wait_ge(f_dv, base + 7)
                        j = 2 * t + s
                        ve.tensor_copy(act[:, 0, bass.ds(j, 1), :], cv[:, :].unsqueeze(1)).then_inc(f_dv, 1)
                        ve.wait_ge(f_dv, base + 8)
                        ve.tensor_tensor(act[:, 1, bass.ds(j, 1), :], cv[:, :].unsqueeze(1),
                                         act[:, 0, bass.ds(j, 1), :].bitcast(F32), ALU.subtract).then_inc(f_dv, 1)
                ve.wait_ge(f_dv, 9 * FT * (l + 1))
                y_start(1 + 2 * l)
                tile0 = plan[f"down{l}"]["t0"]
                with ve.Fori(0, 4) as t:
                    for c in range(6):
                        if l == 0:
                            ada_chunk(6 * t + (24 + c), c % 2, ada_in1, ada_acc1, 3 * t + (12 + c // 2))
                        if c in (1, 4):
                            y_square(1 + 2 * l, tile0, 2 * t + c // 3, c // 3)

            ve.memset(relt[32:33, :], NEG).then_inc(setup, 1)
            ve.memset(one[:, :], 1.0).then_inc(setup, 1)
            for n in range(2):
                ve.memset(ub0[:, n, 0:PAD], 0.0).then_inc(pad, 1)
            ve.wait_ge(const_in, 96)
            ve.tensor_copy(cr[:, :, :].rearrange("p a b -> p (a b)"),
                           dm[:, :, :].rearrange("p a b -> p (a b)")[:, 0:5 * P]).then_inc(setup, 1)
            n = KT * 16
            ve.tensor_copy(wdt[:, 0, 0:n], wdt_f[:, :]).then_inc(setup, 1)
            ve.memset(wdt[:, :, n:].bitcast(F32), 0.0).then_inc(setup, 1)
            ve.wait_ge(setup, 4)
            ve.tensor_tensor(wdt[:, 1, 0:n], wdt_f[:, :], wdt[:, 0, 0:n].bitcast(F32), ALU.subtract).then_inc(setup, 1)
            for n in range(2):
                ve.wait_ge(table_mm, n + 1)
                ve.tensor_copy(table[:, 320 * n:320 * n + 320], ps[0:16, n, 0:320]).then_inc(table_out, 1)
            ve.wait_ge(cond_ready, 1)
            for a in range(ADA_FIRST):
                ada_chunk(a, a % 2, ada_in0, ada_acc0, a // 2)
            modulation(0, 16)
            ve.wait_ge(mod_ready, 1)
            a_gain(0)
            ve.wait_ge(mod_ready, 2)
            ve.wait_ge(x_in, 16)
            norm_in(0)

            def ada_pair(t, at_):
                for s in range(2):
                    ada_chunk(2 * t + (at_ + s), s, ada_in0, ada_acc0, t + at_ // 2)

            for at_ in (8, 10):
                with ve.Fori(0, 1) as t:
                    ada_pair(t, at_)

            def xbc(t):
                for n in range(4):
                    x_ = 4 * t + n
                    ve.wait_ge(evac, x_ + (plan["xbc"]["t0"] + 1))
                    wait(ve, silu_x, x_ - 1)
                    taps(cacc0[:, n % 2], ub0[:, n % 2], lambda j: pc("conv_w", 4 * x_ + j), pc("conv_b", x_), 4,
                         conv, 4 * x_, between=lambda j: ada_step(4 * (n % 2) + j, 2 * t + (12 + n // 2), n // 2, ada_in0,
                                                                  ada_acc0, t + 6))
                    if n % 2:
                        ada_step(KT, 2 * t + (12 + n // 2), n // 2, ada_in0, ada_acc0, t + 6)

            ve.wait_ge(pad, 2)
            xbc(0)
            with ve.Fori(1, 4) as t:
                xbc(t)
            with ve.Fori(0, 2) as t:
                ada_pair(t, 20)
            modulation(16, 48)
            ve.wait_ge(mod_ready, 3)
            g_gain(0)
            a_gain(1)
            g_gain(1)

            def heads(name):
                return par[:, pcol[name][0]:pcol[name][0] + 16]

            def over_tiles(ap):
                return ap.unsqueeze(1).to_broadcast([P, NT, 16])

            ve.wait_ge(dt_mm, 1)
            ve.tensor_copy(acs[:, :], ps[0:16, 6, :]).then_inc(dt_dv, 1)
            ve.wait_ge(dt_mm, 2)
            ve.tensor_tensor(dt_raw, ps[:, 6, 0:64].rearrange("p (t h) -> p t h", t=NT), over_tiles(heads("dt_bias")),
                             ALU.add).then_inc(dt_dv, 1)
            ve.wait_ge(dt_dv, 2)
            ve.scalar_tensor_tensor(dt_l, dt_raw, -1.0, dt_raw, ALU.mult, ALU.min).then_inc(dt_dv, 1)
            ve.wait_ge(dt_ac, 3)
            ve.scalar_tensor_tensor(dt_v, dt_raw, 0.0, dt_l, ALU.max, ALU.add).then_inc(dt_dv, 1)
            ve.tensor_scalar(dts[:, 6, 1, :], dts[:, 6, 0, :], -1.0, None, ALU.mult).then_inc(dt_dv, 1)
            ve.wait_ge(dt_dv, 5)
            ve.tensor_tensor(dt_a, dt_v, over_tiles(dts[:, 6, 1, :]), ALU.mult).then_inc(dt_dv, 1)

            def sb_softplus(u):
                ve.wait_ge(sb_e, 2 * u + 2)
                for n, (at_, w) in enumerate(BANKS):
                    l = sb_l[:, u % 2, at_:at_ + w]
                    ve.scalar_tensor_tensor(l, ps[:, 3 * (u % 2) + n, 0:w], 0.0, l, ALU.max, ALU.add).then_inc(sb_L, 1)
                ve.wait_ge(sb_L, 3 * u + 3)
                if u >= 2:
                    ve.wait_ge(sb_s, 3 * (u - 1))
                ve.tensor_copy(sb_lr[:, u % 2, 0], sb_l[:, u % 2]).then_inc(sb_hi, 1)

            def sb_out(i):
                ve.wait_ge(sb_pv, 2 * i + 2)
                ve.tensor_copy(mix_sb[:, 0, i], ps[:, 6 + i % 2, :]).then_inc(sb_mix, 1)
                ve.wait_ge(sb_mix, 2 * i + 1)
                ve.tensor_tensor(mix_sb[:, 1, i], ps[:, 6 + i % 2, :], mix_sb[:, 0, i].bitcast(F32),
                                 ALU.subtract).then_inc(sb_mix, 1)

            ve.wait_ge(dt_mm, 4)
            ve.tensor_copy(dt_acs, ps[:, 7, 0:64].rearrange("p (t h) -> p t h", t=NT)).then_inc(dt_dv, 1)
            ve.wait_ge(dt_ac, 4)
            ve.tensor_tensor(dt_w, dt_w, dt_v, ALU.mult).then_inc(dt_dv, 1)
            sb_softplus(0)
            ve.wait_ge(dt_tr, 1)
            ve.tensor_copy(acs[:, :], ps[0:16, 6, :]).then_inc(dt_dv, 1)
            sb_softplus(1)
            for u in range(SB_HEADS):
                if u + 2 < SB_HEADS:
                    sb_softplus(u + 2)
                if u >= 2 and u % 2 == 0:
                    sb_out(u // 2 - 1)
            sb_out(3)

            def per_head(i, c0, n, g):
                return dts[:, i, c0:c0 + n, 4 * g:4 * g + 4].unsqueeze(3).to_broadcast([P, n, 4, HD])

            def cols(ap):
                return ap.rearrange("p c (h d) -> p c h d", d=HD)

            def gate_pair(k):
                ve.wait_ge(hd_y, 2 * k + 2)
                col = pcol["d_skip"][0] + k
                ve.scalar_tensor_tensor(yt[:, :], xs[:, k], par[:, col:col + 1], ps[:, 1 + k % 2, :],
                                        ALU.mult, ALU.add).then_inc(yg, 1)
                ve.wait_ge(yg, 3 * k + 1)
                ve.tensor_tensor(zs[:, k], yt[:, :], zs[:, k], ALU.mult).then_inc(yg, 1)

            def add_gated(k):
                ve.wait_ge(ms_sq, k + 1)
                if k == 0:
                    ve.tensor_copy(s_low["ssum"][:, :], s_low["sq"][:, 0]).then_inc(yg, 1)
                else:
                    ve.tensor_tensor(s_low["ssum"][:, :], s_low["ssum"][:, :], s_low["sq"][:, k % 2],
                                     ALU.add).then_inc(yg, 1)

            ve.wait_ge(dt_dv, 9)
            ve.tensor_copy(acs_r[:, 0], acs[:, :]).then_inc(dt_dv, 1)
            ve.wait_ge(dt_dv, 10)
            ve.tensor_tensor(acs_r[:, 1], acs[:, :], acs_r[:, 0].bitcast(F32), ALU.subtract).then_inc(dt_dv, 1)
            for g in range(SSM_GROUPS):
                if g:
                    ve.wait_ge(hd_y, 4 * g)
                for n in range(2):
                    ve.wait_ge(g_pe, 3 * g + 1 + n)
                    src = ps[:, 1 + n, :].rearrange("p (c f) -> p c f", c=2)
                    ve.tensor_tensor(cols(xdt[:, 2 * n:2 * n + 2]), cols(src), per_head(2, 2 * n, 2, g),
                                     ALU.mult).then_inc(g_dv, 1)
                    m = 2 - n
                    ve.tensor_tensor(cols(xw[:, 2 * n:2 * n + m]), cols(src[:, 0:m]), per_head(5, 2 * n, m, g),
                                     ALU.mult).then_inc(g_dv, 1)
                if g:
                    add_gated(2 * g - 1)
                for hh in range(4):
                    n = 4 * g + hh
                    ve.wait_ge(hd_mask, n + 1)
                    if n >= 2:
                        ve.wait_ge(hd_y, n - 1)
                    ve.tensor_tensor(dm[:, n % 2].rearrange("p (c l) -> p c l", c=NT),
                                     ps[:, 6 + n % 2, :].rearrange("p (c l) -> p c l", c=NT),
                                     dt_acs[:, :, n:n + 1].to_broadcast([P, NT, P]), ALU.subtract).then_inc(hd_d, 1)
                    ve.wait_ge(hd_x, n + 1)
                    ve.wait_ge(g_ac, 3 * g + 3)
                    ve.tensor_tensor(dm[:, n % 2], dm[:, n % 2], cb[:, g % 2], ALU.mult).then_inc(hd_dv, 1)
                    ve.tensor_tensor(cs[:, n % 2], xs[:, 12 + g, P:], eb[:, n % 2, P:], ALU.mult).then_inc(hd_dv, 1)
                    for c, (bank, off) in ((1, (4, 256)), (2, (5, 0))):
                        if c == 2:
                            ve.wait_ge(hd_dv, 4 * n + 3)
                        hs = slice(HD * hh, HD * hh + HD)
                        ve.scalar_tensor_tensor(st[:, c, hs], st[:, c - 1, hs],
                                                eb[:, n % 2, P * (c + 1) - 1:P * (c + 1)],
                                                ps[:, bank, off + HD * hh:off + HD * hh + HD],
                                                ALU.mult, ALU.add).then_inc(hd_dv, 1)
                    if hh >= 2:
                        if hh == 3:
                            add_gated(2 * g)
                        gate_pair(2 * g + hh - 2)
            add_gated(7)
            ve.wait_ge(n_rs, RS_SSM + 2)
            for k in range(8):
                col = pcol["ssm_norm"][0] + k
                if k >= HM:
                    ve.wait_ge(ms_lo, k + 1 - HM)
                ve.scalar_tensor_tensor(s_low["hm"][:, k % HM], zs[:, k], par[:, col:col + 1], s_low["rstd"][:, :],
                                        ALU.mult, ALU.mult).then_inc(ms_dv, 1)
                ve.wait_ge(ms_dv, 2 * k + 1)
                ve.tensor_copy(mix_ssm[:, 0, k], s_low["hm"][:, k % HM]).then_inc(ms_dv, 1)

            y_start(0)
            with ve.Fori(0, 4) as t:
                for s in range(2):
                    y_square(0, plan["out0"]["t0"], 2 * t + s, s)
            residual(0)
            norm_in(1)
            ffn(0)
            modulation(48, 96)
            ve.wait_ge(mod_ready, 7)
            for i in (2, 3):
                a_gain(i)
                g_gain(i)
            ve.wait_ge(mod_ready, 11)
            residual(1)

            norm_in(2)
            ve.wait_ge(npar_in, 16)
            n = KT * 48
            src = npar[:, ncol["w_gate"][0]:ncol["w_gate"][0] + n]
            ve.tensor_copy(wg_r[:, 0, 0:n], src).then_inc(gt_w, 1)
            ve.memset(wg_r[:, :, n:].bitcast(F32), 0.0).then_inc(gt_w, 1)
            ve.wait_ge(gt_w, 1)
            ve.tensor_tensor(wg_r[:, 1, 0:n], src, wg_r[:, 0, 0:n].bitcast(F32), ALU.subtract).then_inc(gt_w, 1)
            for kv in range(2):
                ve.wait_ge(shift_in[kv], 128)
                wait(ve, fl_lo, kv)
                for i in range(16):
                    col = ncol["pe"][0] + 16 * kv + i
                    ve.tensor_scalar(fl[:, i, :].rearrange("p (g n) -> p g n", g=NSA_GROUPS),
                                     kcs[:, kv, :, 2 * i:2 * i + 16 * (CMP_N - 1) + 1:16], npar[:, col:col + 1], None,
                                     ALU.add).then_inc(fl_dv, 1)
            ph = plan["w1"]
            for i in range(ph["n"]):
                ve.wait_ge(w_lo, ph["c0"] + i)
                ve.wait_ge(w_hi, ph["c0"] + i + 1 + ph["extra"])
                ve.tensor_tensor(ring[:, i % 2, 1], raw[:, i % 2], ring[:, i % 2, 0].bitcast(F32),
                                 ALU.subtract).then_inc(w_lo, 1)
            ve.wait_ge(c_mm, 1)
            ve.tensor_copy(kcmp[:, :], ps[:, 4, 0:124]).then_inc(a_mx, 1)
            ve.wait_ge(c_mm, 2)
            ve.tensor_copy(vcmp[:, :], ps[0:CMP_N, 5, 0:256]).then_inc(a_mix, 1)
            ve.wait_ge(a_pt, 1)
            ve.tensor_scalar(gates[:, :, :], gates[:, :, :], 1.0, None, ALU.add).then_inc(a_mix, 1)
            ve.wait_ge(a_mix, 2)
            ve.reciprocal(gates[:, :, :], gates[:, :, :]).then_inc(a_mix, 1)
            ve.wait_ge(a_mix, 3)

            def nsa_max(gp, t, u):
                pr, b, r = u // 6, u // 3 % 2, u % 3
                for i, (qt, (at_, w)) in enumerate(nsa_rows(u)):
                    n = (1, 2, 1, 0)[qt] if u % 3 < 2 else 0
                    ve.reg_add(scores, scores_before, 56 * gp + T_BEFORE[u] + n + 2)
                    if i == 0:
                        ve.reg_add(turned, scores_before, 56 * gp + T_BEFORE[max(0, u - 2)] + 1)
                    ve.wait_ge(a_mix, 3)
                    if i == 0:
                        ve.wait_ge(a_t, turned)
                    ve.wait_ge(a_s, scores)
                    bias = u_b[:, pr, b, 384 - P * qt:] if u % 3 < 2 else u_b[:, pr, b, 415 - P * qt::16]
                    ve.tensor_tensor_reduce(s_p[:, r, at_:at_ + w], ps[:, n, at_ - BANKS[n][0]:at_ - BANKS[n][0] + w],
                                            bias, 1.0, -3e38, ALU.add, ALU.max, mx[:, r, qt:qt + 1]).then_inc(a_mx, 1)
                ve.wait_ge(a_mx, 48 * t + (96 * gp + 4 * u + 5))
                ve.tensor_scalar(mx[:, r], mx[:, r], -1.0, 1e29, ALU.mult, ALU.min).then_inc(a_neg, 1)

            def nsa_scale(gp, t, u):
                pr, b, br, r = u // 6, u // 3 % 2, u % 3, u % 3
                ve.wait_ge(a_p, 48 * t + (96 * gp + 4 * u + 4))
                base = 28 * t + (56 * gp + SC_BEFORE[u])
                sums = rs[:, r]
                if br == 2:
                    ve.tensor_scalar(sc[:, r], sums, 1e-30, None, ALU.max).then_inc(a_sc, 1)
                    ve.wait_ge(a_sc, base + 1)
                    base, sums = base + 1, sc[:, r]
                ve.reciprocal(sc[:, r], sums).then_inc(a_sc, 1)
                ve.wait_ge(a_sc, base + 1)
                gate = gates[:, bass.ds(6 * t + (3 * (8 * gp + 4 * b + pr) + (1, 2, 0)[br]), 1), :]
                ve.tensor_tensor(sc[:, r:r + 1], sc[:, r:r + 1], gate, ALU.mult).then_inc(a_sc, 1)
                ve.wait_ge(a_sc, base + 2)
                for qt, (at_, w) in nsa_rows(u):
                    ve.tensor_scalar(s_p[:, r, at_:at_ + w], s_p[:, r, at_:at_ + w], sc[:, r, qt:qt + 1], None,
                                     ALU.mult).then_inc(a_n, 1)

            def nsa_low(gp, t, pr):
                ve.wait_ge(a_hi, 2 * t + (4 * gp + pr + 1))
                j = 2 * t + (4 * gp + pr)
                ve.tensor_tensor(mix1[:, 1, bass.ds(j, 1), :], ps[:, 6 + pr:7 + pr, :],
                                 mix1[:, 0, bass.ds(j, 1), :].bitcast(F32), ALU.subtract).then_inc(a_mix, 1)

            scores_before, scores, turned = (ve.alloc_register(k) for k in ("scores_before", "scores", "turned"))
            for gp in range(2):
                with ve.Fori(0, 2) as t:
                    ve.reg_mul(scores_before, t, 28)
                    ve.wait_ge(a_s, 28 * t + (56 * gp + 1))
                    ve.wait_ge(u_in[0], 16 * t + (32 * gp + 16))
                    for pr in range(2):
                        ve.tensor_copy(q_st[:, pr:pr + 1], f1[:, bass.ds(2 * t + (4 + 4 * gp + pr), 1), :]).then_inc(a_q, 1)
                    for v in range(15):
                        if v < 12:
                            nsa_max(gp, t, v)
                        if v == 5:
                            ve.wait_ge(u_in[1], 16 * t + (32 * gp + 16))
                        if 1 <= v < 13:
                            nsa_scale(gp, t, v - 1)
                        if v in (10, 14):
                            nsa_low(gp, t, v // 14)

            y_start(2)
            with ve.Fori(0, 2) as t:
                for n in range(4):
                    y_square(2, plan["out1"]["t0"], 4 * t + n, n % 2)
            residual(2)
            norm_in(3)
            ffn(1)
            residual(3)


_OUT = (DM, SEQ)


def _layout(i):
    import math

    import numpy as np

    f = np.float32
    eye = np.eye(P, dtype=f)
    p, q = np.arange(P)[:, None], np.arange(P)[None, :]
    consts = np.stack([
        eye, np.full((P, P), 1.0 / DM, f), (p <= q).astype(f), (p > q).astype(f),
        eye, -(p >= q).astype(f), np.full((P, P), -1.0, f),
        np.where(p >= q, f(NEG), f(0)).astype(f), np.where(p > q, f(NEG), f(0)).astype(f)], axis=1)

    dist = np.arange(SEQ)
    nf = np.maximum(dist, 1).astype(f)
    large = np.minimum(16 + (np.log(nf / f(16)) / f(math.log(64)) * f(16)).astype(np.int32), REL_BUCKETS - 1)
    bucket = np.where(dist < 16, dist, large)
    onehot = np.zeros((33, 640), f)
    onehot[bucket[511 - np.arange(SEQ)], np.arange(SEQ)] = 1
    onehot[32, SEQ:] = 1

    def cols(a):
        return a.reshape(-1, P).T

    def put(columns, total, values):
        out = np.zeros((P, total), f)
        for name, v in values.items():
            at, n = columns[name]
            out[:, at:at + n] = v
        return out

    conv_w, fw, fb = i["ab_conv_w"][0], i["ffn_conv_w"], i["ffn_conv_b"]
    pcols, n_p = param_columns()
    params = put(pcols, n_p, {
        "ada_b": cols(i["ada_b"]), "norm_g": cols(i["norm_g"]),
        "conv_w": conv_w.reshape(4, 16, P).transpose(2, 1, 0).reshape(P, 64), "conv_b": cols(i["ab_conv_b"][0]),
        "d_skip": cols(np.repeat(i["ab_d_skip"][0], HD)), "ssm_norm": cols(i["ab_ssm_norm"][0]),
        "fconv_w0": fw[0].reshape(3, 44, P).transpose(2, 1, 0).reshape(P, 132),
        "fconv_w1": fw[1].reshape(3, 44, P).transpose(2, 1, 0).reshape(P, 132),
        "fconv_b0": cols(fb[0]), "fconv_b1": cols(fb[1]),
        "dt_bias": np.broadcast_to(i["ab_dt_bias"][0], (P, 16)), "a_log": np.broadcast_to(i["ab_a_log"][0], (P, 16)),
        "cond": cols(i["c"][0])})

    def out_tiles(w, kt, per):
        n = w.shape[1] // P
        return w.reshape(kt, P, n, P).transpose(2, 1, 0, 3).reshape(n // per, per, P, kt * P).transpose(0, 2, 1, 3) \
            .reshape(n // per, P, per * kt * P)

    def rows512(w):
        return w.reshape(2, 4, P, SEQ).transpose(0, 2, 1, 3).reshape(2, P, CW)

    w_in, w_nsa = i["ab_w_in"][0], i["nsa_w_in"][0]
    f0 = np.concatenate([w_in[:, 0:1024], w_in[:, 2560:4608], w_in[:, 1536:2560]], axis=1)
    w_dt = w_in[:, 4608:4624].reshape(KT, P, 16).transpose(1, 0, 2).reshape(P, KT * 16)
    heads = [8 * (j // 4) + j % 4 + 4 * b for j in range(8) for b in range(2)]
    wq = w_nsa[:, 0:1024].reshape(DM, 16, HD)[:, heads].reshape(DM, 1024)
    f1 = np.concatenate([w_nsa[:, 1024:1536], wq, w_nsa[:, 1536:1792], w_nsa[:, 2048:2304]], axis=1)
    v1 = np.concatenate([w_nsa[:, 1792:2048], w_nsa[:, 2304:2560]], axis=1)
    w_o1 = i["nsa_w_out"][0].reshape(16, HD, DM)[heads].reshape(1024, DM)
    w1, w2, pe = i["nsa_cmp_w1"][0], i["nsa_cmp_w2"][0], i["nsa_cmp_pe"][0]
    w2k = w2[0].reshape(2, P, HD).transpose(1, 0, 2)
    ncols, n_n = nsa_columns()
    nsa_params = put(ncols, n_n, {
        "w2k": np.concatenate([w2k, w2k], axis=2).reshape(P, 256),
        "w2v": w2[1].reshape(2, P, HD).transpose(1, 0, 2).reshape(P, 128),
        "w_gate": w_nsa[:, 2560:2608].reshape(KT, P, 48).transpose(1, 0, 2).reshape(P, 384),
        "pe": pe.reshape(2, 16, P).transpose(2, 0, 1).reshape(P, 32),
        "b1": cols(i["nsa_cmp_b1"][0])})
    up = i["ffn_w_up"].reshape(2, KT, P, 2, FT, P).transpose(0, 4, 2, 3, 1, 5).reshape(2 * FT, P, CW)
    down = i["ffn_w_down"].reshape(2, 2, 11, P, KT, P).transpose(0, 4, 1, 3, 2, 5).reshape(32, P, 11 * P)
    ada = i["ada_w"].reshape(2, KT, P, ADA_N, ADA_W).transpose(0, 3, 2, 1, 4).reshape(2 * ADA_N, P, KT, ADA_W)
    return [
        i["x"][0].T, consts, params, nsa_params, w_dt, onehot, i["rel_bias"].T, ada,
        rows512(w_in[:, 1024:1536]), out_tiles(f0, KT, 2), out_tiles(i["ab_w_out"][0], 12, 1),
        rows512(v1), out_tiles(f1, KT, 2),
        w1.reshape(2, 2, 8, P, 256).transpose(0, 1, 3, 2, 4).reshape(4, P, CW),
        out_tiles(w_o1, KT, 2), up, down]


def kernel(**inputs):
    import numpy as _np
    import concourse.bacc as _bacc
    from concourse import mybir as _mybir
    from concourse.bass_utils import run_bass_kernel_spmd as _run

    nc = _bacc.Bacc("TRN2", target_bir_lowering=False, num_devices=1)
    arrays, args = {}, []
    for n, a in enumerate(_layout({k: _np.asarray(v) for k, v in inputs.items()})):
        a = _np.ascontiguousarray(a)
        arrays[f"in_{n}_dram"] = a
        args.append(nc.dram_tensor(f"in_{n}_dram", a.shape, _mybir.dt.from_np(a.dtype), kind="ExternalInput").ap())
    out = nc.dram_tensor("out_0_dram", _OUT, _mybir.dt.float32, kind="ExternalOutput").ap()
    trunk(nc, *args, out)
    r = _run(nc, [arrays], core_ids=[0])
    return _np.ascontiguousarray(r.results[0]["out_0_dram"].T)[None]
```
